# Optimizing a Trainium2 kernel written in Bass

```python
import math
import jax
import jax.numpy as jnp
from jax import lax
import numpy as np

D_MODEL = 1024
BATCH = 1
SEQ = 1024
DEPTH = 2

PLE_DIM = 256
N_MIXERS = 2
HEAD_DIM = 64
N_HEADS = D_MODEL // HEAD_DIM
ATTN_WIDTH = N_HEADS * HEAD_DIM
WIN_DIL = ((128, 1), (512, 4), (2048, 16))
N_GROUPS = len(WIN_DIL)
ROPE_THETA = 10000.0
CONV_WIDTH = 31
CONV_CH = D_MODEL
RMS_EPS = 1e-6
LN_EPS = 1e-5
NEG_INF = -1e30
ATTN_IN_COLS = 3 * N_GROUPS * ATTN_WIDTH + ATTN_WIDTH
CONV_IN_COLS = 3 * CONV_CH
N_ATTN_LAYERS = (DEPTH + 1) // 2
N_CONV_LAYERS = DEPTH // 2

kernel_name = "hybrid_dilated_attn_conformer_trunk"

def _rmsnorm(x, g):
    xf = x.astype(jnp.float32)
    y = xf * lax.rsqrt(jnp.mean(xf * xf, axis=-1, keepdims=True) + RMS_EPS)
    return (y * g.astype(jnp.float32)).astype(x.dtype)

def _layernorm(x, g, b):
    xf = x.astype(jnp.float32)
    mu = jnp.mean(xf, axis=-1, keepdims=True)
    var = jnp.mean(jnp.square(xf - mu), axis=-1, keepdims=True)
    y = (xf - mu) * lax.rsqrt(var + LN_EPS)
    return (y * g.astype(jnp.float32) + b.astype(jnp.float32)).astype(x.dtype)

def _rope_tables(positions):
    inv_freq = 1.0 / (ROPE_THETA ** (jnp.arange(0, HEAD_DIM, 2, dtype=jnp.float32) / HEAD_DIM))
    ang = positions.astype(jnp.float32)[..., None] * inv_freq
    return jnp.cos(ang)[:, :, None, None, :], jnp.sin(ang)[:, :, None, None, :]

def _apply_rope(t, cos, sin):
    tf = t.astype(jnp.float32)
    t1, t2 = jnp.split(tf, 2, axis=-1)
    out = jnp.concatenate([t1 * cos - t2 * sin, t2 * cos + t1 * sin], axis=-1)
    return out.astype(t.dtype)

def _dilated_window_attention(q, k, v, dilation, n_back):
    B, S, H, E = q.shape
    L = S // dilation
    nb = -(-L // n_back)
    Lp = nb * n_back

    def to_blocks(t):
        t = t.reshape(B, L, dilation, H, E).transpose(0, 2, 1, 3, 4)
        t = jnp.pad(t, ((0, 0), (0, 0), (0, Lp - L), (0, 0), (0, 0)))
        return t.reshape(B, dilation, nb, n_back, H, E)

    def with_prev(t):
        prev = jnp.pad(t, ((0, 0), (0, 0), (1, 0), (0, 0), (0, 0), (0, 0)))[:, :, :-1]
        return jnp.concatenate([prev, t], axis=3)

    qb = to_blocks(q)
    kk = with_prev(to_blocks(k))
    vv = with_prev(to_blocks(v))

    s = jnp.einsum('brnqhe,brnkhe->brnhqk', qb, kk).astype(jnp.float32) * (E ** -0.5)
    qi = jnp.arange(n_back)[:, None]
    kj = jnp.arange(2 * n_back)[None, :]
    dist = n_back + qi - kj
    band = (dist >= 0) & (dist <= n_back)
    has_prev = (jnp.arange(nb) > 0)[:, None, None] | (kj >= n_back)[None]
    valid = band[None] & has_prev
    s = jnp.where(valid[None, None, :, None, :, :], s, NEG_INF)
    lse = jax.nn.logsumexp(s, axis=-1)
    prob = jnp.exp(s - lse[..., None])
    o = jnp.einsum('brnhqk,brnkhe->brnqhe', prob.astype(vv.dtype), vv).astype(jnp.float32)

    o = o.reshape(B, dilation, Lp, H, E)[:, :, :L].transpose(0, 2, 1, 3, 4).reshape(B, S, H, E)
    lse = lse.transpose(0, 1, 2, 4, 3).reshape(B, dilation, Lp, H)[:, :, :L]
    lse = lse.transpose(0, 2, 1, 3).reshape(B, S, H)
    return o, lse

def _attention_branch(h, w_in, w_out, cos, sin):
    B, S, _ = h.shape
    proj = h @ w_in.astype(h.dtype)
    qkv = proj[..., :3 * N_GROUPS * ATTN_WIDTH].reshape(B, S, 3, N_GROUPS, N_HEADS, HEAD_DIM)
    z = proj[..., 3 * N_GROUPS * ATTN_WIDTH:]
    q = _apply_rope(qkv[:, :, 0], cos, sin)
    k = _apply_rope(qkv[:, :, 1], cos, sin)
    v = qkv[:, :, 2]
    outs, lses = [], []
    for g, (window, dilation) in enumerate(WIN_DIL):
        o_g, lse_g = _dilated_window_attention(q[:, :, g], k[:, :, g], v[:, :, g],
                                               dilation, window // dilation)
        outs.append(o_g)
        lses.append(lse_g)
    wts = jax.nn.softmax(jnp.stack(lses, axis=0), axis=0)
    o = jnp.sum(wts[..., None] * jnp.stack(outs, axis=0), axis=0)
    o = o.reshape(B, S, ATTN_WIDTH).astype(h.dtype)
    return (o * jax.nn.silu(z)) @ w_out.astype(h.dtype)

def _conv_branch(h, w_in, dw_w, dw_b, ln_g, ln_b, w_out):
    proj = h @ w_in.astype(h.dtype)
    a, b, z = jnp.split(proj, 3, axis=-1)
    u = a * jax.nn.sigmoid(b)
    u = lax.conv_general_dilated(
        u, dw_w.astype(u.dtype)[:, None, :],
        window_strides=(1,), padding=((CONV_WIDTH - 1, 0),),
        dimension_numbers=('NWC', 'WIO', 'NWC'),
        feature_group_count=CONV_CH) + dw_b.astype(u.dtype)
    u = jax.nn.silu(_layernorm(u, ln_g, ln_b))
    return (u * jax.nn.silu(z)) @ w_out.astype(h.dtype)

def setup_inputs(seed: int = 0) -> dict:
    key = jax.random.key(seed)
    ks = jax.random.split(key, 16)
    nrm = jax.random.normal
    f32 = jnp.float32
    x = nrm(ks[0], (BATCH, SEQ, D_MODEL), f32)
    p = nrm(ks[1], (DEPTH, BATCH, SEQ, PLE_DIM), f32)
    offset = jax.random.randint(ks[2], (BATCH, 1), 0, SEQ, dtype=jnp.int32)
    positions = jnp.arange(SEQ, dtype=jnp.int32)[None, :] + offset
    pre_norm_g = 1.0 + 0.05 * nrm(ks[3], (DEPTH, D_MODEL), f32)
    post_norm_g = 1.0 + 0.05 * nrm(ks[4], (DEPTH, D_MODEL), f32)
    attn_w_in = nrm(ks[5], (N_ATTN_LAYERS, D_MODEL, ATTN_IN_COLS), f32) * D_MODEL ** -0.5
    attn_w_out = nrm(ks[6], (N_ATTN_LAYERS, ATTN_WIDTH, D_MODEL), f32) * ATTN_WIDTH ** -0.5
    conv_w_in = nrm(ks[7], (N_CONV_LAYERS, D_MODEL, CONV_IN_COLS), f32) * D_MODEL ** -0.5
    conv_dw_w = nrm(ks[8], (N_CONV_LAYERS, CONV_WIDTH, CONV_CH), f32) * CONV_WIDTH ** -0.5
    conv_dw_b = 0.02 * nrm(ks[9], (N_CONV_LAYERS, CONV_CH), f32)
    conv_ln_g = 1.0 + 0.05 * nrm(ks[10], (N_CONV_LAYERS, CONV_CH), f32)
    conv_ln_b = 0.02 * nrm(ks[11], (N_CONV_LAYERS, CONV_CH), f32)
    conv_w_out = nrm(ks[12], (N_CONV_LAYERS, CONV_CH, D_MODEL), f32) * CONV_CH ** -0.5
    ple_w_proj = nrm(ks[13], (DEPTH, PLE_DIM, D_MODEL), f32) * PLE_DIM ** -0.5
    ple_w_gate = nrm(ks[14], (DEPTH, D_MODEL, D_MODEL), f32) * D_MODEL ** -0.5
    return {"x": x, "p": p, "positions": positions,
            "pre_norm_g": pre_norm_g, "post_norm_g": post_norm_g,
            "attn_w_in": attn_w_in, "attn_w_out": attn_w_out,
            "conv_w_in": conv_w_in, "conv_dw_w": conv_dw_w, "conv_dw_b": conv_dw_b,
            "conv_ln_g": conv_ln_g, "conv_ln_b": conv_ln_b, "conv_w_out": conv_w_out,
            "ple_w_proj": ple_w_proj, "ple_w_gate": ple_w_gate}

def reference(x, p, positions, pre_norm_g, post_norm_g, attn_w_in, attn_w_out,
              conv_w_in, conv_dw_w, conv_dw_b, conv_ln_g, conv_ln_b, conv_w_out,
              ple_w_proj, ple_w_gate):
    cos, sin = _rope_tables(positions)
    for i in range(DEPTH):
        h = _rmsnorm(x, pre_norm_g[i])
        j = i // N_MIXERS
        if i % N_MIXERS == 0:
            y = _attention_branch(h, attn_w_in[j], attn_w_out[j], cos, sin)
        else:
            y = _conv_branch(h, conv_w_in[j], conv_dw_w[j], conv_dw_b[j],
                             conv_ln_g[j], conv_ln_b[j], conv_w_out[j])
        x = x + _rmsnorm(y, post_norm_g[i])
        x = x + (p[i].astype(x.dtype) @ ple_w_proj[i].astype(x.dtype)) * \
            jax.nn.sigmoid(x @ ple_w_gate[i].astype(x.dtype))
    return x


_drawn_inputs = setup_inputs


def setup_inputs(seed=0):
    import zlib

    import numpy as np

    out = dict(_drawn_inputs(seed))
    spreads = {}
    factors = {'conv_dw_b': 2.687, 'conv_ln_b': 5.144}
    for name, (base, spread) in spreads.items():
        noise = np.random.default_rng([zlib.crc32(name.encode()), seed]).standard_normal(out[name].shape)
        drawn = base * np.exp(spread * noise) if base else spread * noise
        out[name] = jnp.asarray(drawn.astype(out[name].dtype))
    for name, factor in factors.items():
        out[name] = (out[name] * factor).astype(out[name].dtype)
    return out
```

```python
from contextlib import ExitStack

import numpy as np
import concourse.bass as bass
from concourse import mybir

F32 = mybir.dt.float32
F32R = mybir.dt.float32r
I32 = mybir.dt.int32
ACT = mybir.ActivationFunctionType
ALU = mybir.AluOpType
AXX = mybir.AxisListType.X

P = 128
SEQ, DM = 1024, 1024
NT = SEQ // P
KC = DM // P
HALF = 512
PLE = 256
HD = 64
HPAIRS = DM // (2 * HD)
NG = 3
DILATION = (1, 4, 16)
LONE = ((0,), (0, 2, 4, 6), tuple(range(8)))
SCALE = HD ** -0.5
NEG = -1e30
THETA = 10000.0
RMS_EPS, LN_EPS = 1e-6, 1e-5
TAPS = 31
UROW = 2 * HD + 4
TWO_PI = 2 * np.pi
PI_A = 6.28125
PI_B = float(np.float32(np.round((TWO_PI - PI_A) * 2 ** 20) / 2 ** 20))
PI_C = float(np.float32(TWO_PI - PI_A - PI_B))
ROUND = 1.5 * 2 ** 23
PI_IN = 3.1415925


def wait(eng, sem, value):
    if isinstance(value, int) and value <= 0:
        return
    eng.wait_ge(sem, value)


def column(eng, value):
    return value if isinstance(value, int) else eng.snap(value)


def f(ap):
    return ap.bitcast(F32)


class Memory:

    def __init__(self, nc, ctx, prefix):
        self.nc, self.ctx, self.prefix, self.sems = nc, ctx, prefix, []

    def sb(self, name, shape, dt=F32):
        return self.ctx.enter_context(self.nc.sbuf_tensor(f"{self.prefix}_{name}", shape, dt))

    def ps(self, name, cols=HALF):
        return self.ctx.enter_context(self.nc.psum_tensor(f"{self.prefix}_{name}", [P, cols], F32))

    def sem(self, name):
        self.sems.append(self.ctx.enter_context(self.nc.semaphore(f"{self.prefix}_{name}")))
        return self.sems[-1]

    def clear(self):
        with self.nc.Block(no_gpsimd_drain=True) as block:
            @block.sync
            def _(sp):
                for s in self.sems:
                    sp.sem_clear(s)


def three_passes(pe, out, lhs_hi, lhs_lo, rhs_hi, rhs_lo, first=True, last=True):
    pe.matmul(out, lhs_hi, rhs_hi, start=first, stop=False)
    pe.matmul(out, lhs_hi, rhs_lo, start=False, stop=False)
    return pe.matmul(out, lhs_lo, rhs_hi, start=False, stop=last)


class PreNorm:
    def __init__(self, m, x, gain, h, banks, ident, minus_half):
        self.x, self.gain, self.h, self.banks, self.ident, self.minus_half = x, gain, h, banks, ident, minus_half
        self.squares = m.sb("pn_squares", [P, DM])
        self.ssq = m.sb("pn_ssq", [P, NT])
        self.rstd = m.sb("pn_rstd", [P, NT])
        self.xn = [m.sb(f"pn_xn{i}", [P, DM]) for i in range(2)]
        self.s_ssq = m.sem("pn_ssq_done")
        self.s_var = m.sem("pn_var_done")
        self.s_rstd = m.sem("pn_rstd_done")
        self.s_xn = m.sem("pn_xn_done")
        self.s_tr = m.sem("pn_transposed")
        self.s_hi = m.sem("pn_hi_done")
        self.s_lo = m.sem("pn_lo_done")

    def act_squares(self, act, t):
        wait(act, self.s_ssq, t)
        act.activation(self.squares[:], self.x[:, t, :], ACT.Square, accum_out=self.ssq[:, t:t + 1]).then_inc(self.s_ssq, 1)

    def pool_rstd(self, pool, t):
        pool.wait_ge(self.s_ssq, t + 1)
        c = slice(t, t + 1)
        pool.tensor_scalar(self.rstd[:, c], self.ssq[:, c], 1.0 / DM, RMS_EPS, ALU.mult, ALU.add).then_inc(self.s_var, 1)
        pool.wait_ge(self.s_var, t + 1)
        pool.tensor_tensor(self.rstd[:, c], self.rstd[:, c], self.minus_half, ALU.pow).then_inc(self.s_rstd, 1)

    def dve_scale(self, dve, t):
        dve.wait_ge(self.s_rstd, t + 1)
        wait(dve, self.s_tr, 2 * (t - 1))
        dve.scalar_tensor_tensor(self.xn[t % 2][:], self.x[:, t, :], self.rstd[:, t:t + 1], self.gain[:],
                                 ALU.mult, ALU.mult).then_inc(self.s_xn, 1)

    def pe_transposes(self, pe, t):
        pe.wait_ge(self.s_xn, t + 1)
        for half in range(2):
            n = 2 * t + half
            wait(pe, self.s_lo, n - 1)
            for k in range(4):
                c = 4 * half + k
                last = pe.transpose(self.banks[half][:, k * P:(k + 1) * P], self.xn[t % 2][:, c * P:(c + 1) * P], self.ident[:])
            last.then_inc(self.s_tr, 1)

    def act_hi(self, act, t):
        for half in range(2):
            act.wait_ge(self.s_tr, 2 * t + half + 1)
            act.activation(self.h[0][:, 4 * half:4 * half + 4, t * P:(t + 1) * P],
                           self.banks[half][:].rearrange("p (k n) -> p k n", k=4), ACT.Copy).then_inc(self.s_hi, 1)

    def dve_lo(self, dve, t):
        for half in range(2):
            dve.wait_ge(self.s_hi, 2 * t + half + 1)
            sl = (slice(None), slice(4 * half, 4 * half + 4), slice(t * P, (t + 1) * P))
            dve.tensor_tensor(self.h[1][sl], self.banks[half][:].rearrange("p (k n) -> p k n", k=4),
                              f(self.h[0][sl]), ALU.subtract).then_inc(self.s_lo, 1)


def setup(nc, a, keep):
    with ExitStack() as ctx:
        m = Memory(nc, ctx, "su")
        x = m.sb("x", [P, NT, DM])
        gain = m.sb("gain", [P, DM])
        pos_i = m.sb("pos_i", [P, NT], I32)
        pos = m.sb("pos", [P, NT])
        inv_freq = m.sb("inv_freq", [P, HD // 2])
        angle = m.sb("angle", [P, NT, HD // 2])
        turns = m.sb("turns", [P, 2, NT, HD // 2])
        p_in = m.sb("p_in", [P, NT, PLE])
        pT = [m.sb(f"pT_{w}", [P, PLE // P, SEQ], F32R) for w in ("hi", "lo")]
        w_raw = m.sb("w_raw", [P, PLE // P, DM])
        w = [m.sb(f"w_{n}", [P, PLE // P, DM], F32R) for n in ("hi", "lo")]
        out = [m.sb(f"out{i}", [P, HALF]) for i in range(4)]
        bank_t = [m.ps(f"bank_t{i}") for i in range(2)]
        bank_p = [m.ps(f"bank_p{i}") for i in range(2)]
        bank_o = [m.ps(f"bank_o{i}") for i in range(4)]
        s_const = m.sem("constants_set")
        s_cchain = m.sem("constants_chain")
        s_pos = m.sem("positions_in")
        s_gain = m.sem("gain_in")
        s_x = [m.sem(f"x_in{t}") for t in range(NT)]
        s_p = m.sem("p_in")
        s_w = m.sem("w_in")
        s_rope = m.sem("rope_chain")
        s_sin = m.sem("sines_done")
        s_pt = m.sem("p_transposed")
        s_phi = m.sem("p_hi_done")
        s_plo = m.sem("p_lo_done")
        s_whi = m.sem("w_hi_done")
        s_wlo = m.sem("w_lo_done")
        s_mm = m.sem("products_done")
        s_out = m.sem("products_copied")
        s_st = [m.sem(f"product_stored{i}") for i in range(4)]
        pn = PreNorm(m, x, gain, keep.h, bank_t, keep.ident, keep.minus_half[:, 0:1])
        DEPTH = 2

        with nc.Block() as block:
            @block.sync
            def _(sp):
                sp.dma_start(pos_i[:], a.positions.rearrange("b (t p) -> p (b t)", p=P), allow_slow_non_contiguous=True).then_inc(s_pos, 16)
                sp.dma_start(gain[:], a.pre_norm_g[0, :].partition_broadcast(P)).then_inc(s_gain, 16)
                for t in range(NT):
                    sp.dma_start(x[:, t, :], a.x[0, t * P:(t + 1) * P, :]).then_inc(s_x[t], 16)
                for l in range(DEPTH):
                    if l:
                        sp.wait_ge(s_pt, 8 * l)
                        sp.wait_ge(s_wlo, 2 * l)
                    sp.dma_start(p_in[:], a.p[l, 0].rearrange("(t p) c -> p t c", p=P)).then_inc(s_p, 16)
                    sp.dma_start(w_raw[:], a.ple_w_proj[l].rearrange("(k p) c -> p k c", p=P)).then_inc(s_w, 16)
                    for n in range(2 * NT):
                        i = 2 * NT * l + n
                        sp.wait_ge(s_out, i + 1)
                        t, half = n // 2, n % 2
                        sp.dma_start(a.pp[l, t * P:(t + 1) * P, half * HALF:(half + 1) * HALF], out[i % 4][:]).then_inc(s_st[i % 4], 16)
                for i in range(4):
                    sp.wait_ge(s_st[i], 16 * DEPTH * NT // 2)

            @block.gpsimd
            def _(pool):
                pool.memset(keep.minus_half[:], -0.5).then_inc(s_const, 1)
                pool.memset(keep.ident[:], 0.0).then_inc(s_cchain, 1)
                pool.memset(keep.band[:], 0.0).then_inc(s_cchain, 1)
                pool.memset(keep.diag[:], 0.0).then_inc(s_cchain, 1)
                pool.wait_ge(s_cchain, 3)
                pool.affine_select(out=keep.ident[:], in_=keep.ident[:], compare_op=ALU.not_equal, fill=1.0,
                                   base=0, pattern=[[-1, P]], channel_multiplier=1).then_inc(s_const, 1)
                pool.affine_select(out=keep.band[:], in_=keep.band[:], compare_op=ALU.is_ge, fill=NEG,
                                   base=P, pattern=[[-1, 2 * P]], channel_multiplier=1).then_inc(s_cchain, 1)
                pool.affine_select(out=keep.diag[:], in_=keep.diag[:], compare_op=ALU.is_ge, fill=NEG,
                                   base=0, pattern=[[-1, P]], channel_multiplier=1).then_inc(s_cchain, 1)
                pool.wait_ge(s_cchain, 5)
                pool.affine_select(out=keep.band[:], in_=keep.band[:], compare_op=ALU.is_ge, fill=NEG,
                                   base=0, pattern=[[1, 2 * P]], channel_multiplier=-1)
                pool.affine_select(out=keep.diag[:, 0:HD], in_=keep.diag[:, 0:HD], compare_op=ALU.is_ge, fill=NEG,
                                   base=HD - 1, pattern=[[0, HD]], channel_multiplier=-1)
                for i in range(HD // 2):
                    v = float(np.float32(1.0) / np.float32(THETA ** (2 * i / HD)))
                    last = pool.memset(inv_freq[:, i:i + 1], v)
                last.then_inc(s_const, 1)
                for t in range(NT):
                    pn.pool_rstd(pool, t)

            @block.vector
            def _(dve):
                n = [0]

                def link(op):
                    n[0] += 1
                    op.then_inc(s_rope, 1)
                    dve.wait_ge(s_rope, n[0])

                dve.wait_ge(s_pos, 16)
                dve.wait_ge(s_const, 3)
                link(dve.tensor_copy(pos[:], pos_i[:]))
                for t in range(NT):
                    last = dve.tensor_scalar(angle[:, t, :], inv_freq[:], pos[:, t:t + 1], None, ALU.mult)
                link(last)
                for q in range(2):
                    link(dve.tensor_scalar(turns[:, q], angle[:], 1.0 / TWO_PI, 0.25 * q, ALU.mult, ALU.add))
                    link(dve.tensor_scalar(turns[:, q], turns[:, q], ROUND, None, ALU.add))
                    link(dve.tensor_scalar(turns[:, q], turns[:, q], ROUND, None, ALU.subtract))
                    rest = keep.rope[:, q]
                    link(dve.scalar_tensor_tensor(rest, turns[:, q], -PI_A, angle[:], ALU.mult, ALU.add))
                    link(dve.scalar_tensor_tensor(rest, turns[:, q], -PI_B, rest, ALU.mult, ALU.add))
                    link(dve.scalar_tensor_tensor(rest, turns[:, q], -PI_C, rest, ALU.mult, ALU.add))
                    link(dve.tensor_scalar(rest, rest, float(q * np.pi / 2), PI_IN, ALU.add, ALU.min))
                    link(dve.tensor_scalar(rest, rest, -PI_IN, None, ALU.max))
                dve.wait_ge(s_gain, 16)
                for l in range(DEPTH):
                    dve.wait_ge(s_whi, 2 * l + 2)
                    for k in range(2):
                        dve.tensor_tensor(w[1][:, k, :], w_raw[:, k, :], f(w[0][:, k, :]), ALU.subtract).then_inc(s_wlo, 1)
                    for t in range(NT):
                        dve.wait_ge(s_phi, NT * l + t + 1)
                        dve.tensor_tensor(pT[1][:, :, t * P:(t + 1) * P], bank_p[t % 2][:, 0:2 * P].rearrange("p (k n) -> p k n", k=2),
                                          f(pT[0][:, :, t * P:(t + 1) * P]), ALU.subtract).then_inc(s_plo, 1)
                        if l == 0:
                            pn.dve_scale(dve, t)
                            if t >= 1:
                                pn.dve_lo(dve, t - 1)
                    if l == 0:
                        pn.dve_lo(dve, NT - 1)

            @block.scalar
            def _(act):
                def squares(t):
                    act.wait_ge(s_x[t], 16)
                    pn.act_squares(act, t)

                for l in range(DEPTH):
                    act.wait_ge(s_w, 16 * (l + 1))
                    if l:
                        act.wait_ge(s_mm, 2 * NT * l)
                    for k in range(2):
                        act.activation(w[0][:, k, :], w_raw[:, k, :], ACT.Copy).then_inc(s_whi, 1)
                    if l == 0:
                        squares(0)
                    for t in range(NT):
                        act.wait_ge(s_pt, NT * l + t + 1)
                        act.activation(pT[0][:, :, t * P:(t + 1) * P], bank_p[t % 2][:, 0:2 * P].rearrange("p (k n) -> p k n", k=2),
                                       ACT.Copy).then_inc(s_phi, 1)
                        if l == 0:
                            if t + 1 < NT:
                                squares(t + 1)
                            if t >= 1:
                                pn.act_hi(act, t - 1)
                        for half in range(2):
                            i = 2 * (NT * l + t) + half
                            act.wait_ge(s_mm, i + 1)
                            wait(act, s_st[i % 4], 16 * (i // 4))
                            act.activation(out[i % 4][:], bank_o[i % 4][:], ACT.Copy).then_inc(s_out, 1)
                    if l == 0:
                        pn.act_hi(act, NT - 1)
                act.wait_ge(s_rope, 18)
                act.activation(keep.rope[:], keep.rope[:], ACT.Sin).then_inc(s_sin, 1)

            @block.tensor
            def _(pe):
                pe.wait_ge(s_const, 2)

                def p_transposes(l, t):
                    n = NT * l + t
                    pe.wait_ge(s_p, 16 * (l + 1))
                    wait(pe, s_plo, n - 1)
                    for k in range(2):
                        last = pe.transpose(bank_p[t % 2][:, k * P:(k + 1) * P], p_in[:, t, k * P:(k + 1) * P], keep.ident[:])
                    last.then_inc(s_pt, 1)

                for l in range(DEPTH):
                    p_transposes(l, 0)
                    pe.wait_ge(s_wlo, 2 * l + 2)
                    for t in range(NT):
                        if t + 1 < NT:
                            p_transposes(l, t + 1)
                        if l == 0:
                            if t >= 1:
                                pn.pe_transposes(pe, t - 1)
                        pe.wait_ge(s_plo, NT * l + t + 1)
                        for half in range(2):
                            i = 2 * (NT * l + t) + half
                            wait(pe, s_out, i - 3)
                            for k in range(2):
                                last = three_passes(pe, bank_o[i % 4][:], pT[0][:, k, t * P:(t + 1) * P], pT[1][:, k, t * P:(t + 1) * P],
                                                    w[0][:, k, half * HALF:(half + 1) * HALF], w[1][:, k, half * HALF:(half + 1) * HALF],
                                                    first=k == 0, last=k == 1)
                            last.then_inc(s_mm, 1)
                    if l == 0:
                        pn.pe_transposes(pe, NT - 1)
        m.clear()


def attention(nc, a, keep):
    h_hi, h_lo = keep.h
    with ExitStack() as ctx:
        m = Memory(nc, ctx, "at")
        raw = [m.sb(f"raw{i}", [P, KC, P]) for i in range(2)]
        wqk = [m.sb(f"wqk_{n}", [P, KC, 2 * P], F32R) for n in ("hi", "lo")]
        wv = [[m.sb(f"wv{i}_{n}", [P, KC, P], F32R) for n in ("hi", "lo")] for i in range(2)]
        qk = [[m.sb(f"qk{g}_{n}", [P, 2, SEQ], F32R) for n in ("hi", "lo")] for g in range(NG)]
        vT = m.sb("vT", [P, SEQ])
        v = [m.sb(f"v_{n}", [P, NT, P], F32R) for n in ("hi", "lo")]
        turned = [m.sb(f"turned{i}", [P, 2, 2 * P]) for i in range(2)]
        rotated = [m.sb(f"rotated{i}", [P, 2 * P]) for i in range(2)]
        prob = [m.sb(f"prob{i}", [P, 2, 2 * P]) for i in range(2)]
        probT = [[m.sb(f"probT{i}_{n}", [P, 4, P], F32R) for n in ("hi", "lo")] for i in range(2)]
        bias = [m.sb(f"bias{i}", [P, 2]) for i in range(2)]
        urow = [m.sb(f"urow{i}", [P, UROW]) for i in range(4)]
        mix = [m.sb(f"mix{q}", [P, 4 * NG, UROW]) for q in range(2)]
        mmax = m.sb("mmax", [P, 4, 2])
        mw = m.sb("mw", [P, 4, NG, 2])
        msw = m.sb("msw", [P, 4, NG, 2])
        mden = m.sb("mden", [P, 4, 2])
        siluz = m.sb("siluz", [P, SEQ])
        bank_p = [m.ps(f"bank_p{i}") for i in range(2)]
        bank_s = m.ps("bank_s", 2 * HALF)
        bank_pt = m.ps("bank_pt")
        bank_o = m.ps("bank_o")
        bank_qk = m.ps("bank_qk")
        bank_vo = m.ps("bank_vo")

        s_raw = [m.sem(f"raw_in{i}") for i in range(2)]
        s_whi = m.sem("w_hi_done")
        s_wlo = m.sem("w_lo_done")
        s_qkp = m.sem("qk_projected")
        s_vp = m.sem("v_projected")
        s_zp = m.sem("z_projected")
        s_turn = m.sem("qk_turned")
        s_rot1 = m.sem("qk_rotated_half")
        s_rot = m.sem("qk_rotated")
        s_qkt = m.sem("qk_transposed")
        s_qkhi = m.sem("qk_hi_done")
        s_qklo = m.sem("qk_lo_done")
        s_vT = m.sem("v_copied")
        s_vt = m.sem("v_transposed")
        s_vhi = m.sem("v_hi_done")
        s_vlo = m.sem("v_lo_done")
        s_ez = m.sem("z_exp_done")
        s_zchain = m.sem("z_chain")
        s_z = m.sem("z_silu_done")
        s_sc = m.sem("scores_done")
        s_mask = m.sem("scores_masked")
        s_max = m.sem("max_done")
        s_bias = m.sem("bias_done")
        s_exp = m.sem("exp_done")
        s_ptr = m.sem("prob_transposed")
        s_pthi = m.sem("probT_hi_done")
        s_ptlo = m.sem("probT_lo_done")
        s_pv = m.sem("pv_done")
        s_u = m.sem("urow_done")
        s_ust = [m.sem(f"urow_stored{i}") for i in range(4)]
        s_stored = m.sem("pair_stored")
        s_mix = [m.sem(f"mix_in{q}") for q in range(2)]
        s_mc = m.sem("mix_chain")
        s_md = m.sem("mix_difference_done")
        s_mw = m.sem("mix_weights_exp")
        s_mcoef = m.sem("mix_coefficients_done")
        s_mm = m.sem("mix_products_done")
        s_ma = m.sem("mix_first_sum_done")
        s_mo = m.sem("mixed")
        s_ot = m.sem("mixed_transposed")
        s_oz = m.sem("gated")
        s_ozst = m.sem("gated_stored")

        NCH = 10
        COL = [0, 3 * DM, 6 * DM, DM, 4 * DM, 7 * DM, 2 * DM, 5 * DM, 8 * DM, 9 * DM]
        PLACE = [(wqk, 0), (wqk, P), (wv[0], 0), (wqk, 0), (wqk, P), (wv[1], 0), (wqk, 0), (wqk, P), (wv[0], 0), (wv[1], 0)]
        w_in = a.attn_w_in[0].rearrange("(k p) c -> p k c", p=P)

        def prev_blocks(g, b):
            return (1,) if b in LONE[g] else (0, 1)

        def perm2(buf, g, start, n):
            d = DILATION[g]
            return buf.rearrange("p (r m) -> p m r", r=d)[:, start // d:(start + n) // d, :]

        def perm3(buf, g, start, n):
            d = DILATION[g]
            return buf.rearrange("p x (r m) -> p x m r", r=d)[:, :, start // d:(start + n) // d, :]

        def rows(hp, g, b):
            d = DILATION[g]
            base = a.u[bass.ds(hp, 1), g]
            r = base.rearrange("h (m r) c -> (h r) m c", r=d)
            L = SEQ // d
            if L >= P:
                return r[(P * b) // L, (P * b) % L:(P * b) % L + P, :]
            return r[P // L * b:P // L * (b + 1)]

        def bodies(eng, body):
            body(0, first=True)
            body(1)
            with eng.Fori(2, HPAIRS - 1) as hp:
                body(hp)
            body(HPAIRS - 1, last=True)
            body(HPAIRS, after=True)

        with nc.Block() as block:
            @block.sync
            def _(sp):
                def load(hp, j):
                    if j >= NCH:
                        hp, j = hp + 1, j - NCH
                    at = column(sp, hp * P + COL[j])
                    wait(sp, s_wlo, NCH * hp + j - 1)
                    sp.dma_start(raw[j % 2][:], w_in[:, :, bass.ds(at, P)]).then_inc(s_raw[j % 2], 16)

                def store(hp, g, b):
                    hp, g = (hp - 1, 2) if g == 0 else (hp, g - 1)
                    pair = column(sp, hp)
                    sp.wait_ge(s_u, NT * (NG * hp + g) + b + 1)
                    sp.dma_start(rows(pair, g, b), urow[b % 4][:]).then_inc(s_ust[b % 4], 16)

                def body(hp, first=False, last=False, after=False):
                    proj = not after
                    for g in range(NG if proj else 2):
                        att = not (first and g == 0) and not (after and g > 0)
                        if proj:
                            load(hp, 3 * g + 3)
                        for s in range(NT):
                            if proj and s == 3 and not (last and g == 2):
                                load(hp, 3 * g + 4)
                            if g == 2 and s == 5 and not last:
                                load(hp, 11)
                            if att and s >= 3:
                                store(hp, g, s - 3)
                        if g < 2 and proj:
                            load(hp, 3 * g + 5)
                        elif proj and not last:
                            load(hp, 12)
                        if att:
                            for b in range(NT - 3, NT):
                                store(hp, g, b)
                        if g == 0 and not first:
                            pair = column(sp, hp - 1)
                            for i in range(4):
                                sp.wait_ge(s_ust[i], 16 * 2 * NG * hp)
                            sp.sem_inc(s_stored, 1)
                            for q in range(2):
                                for t in range(4):
                                    sp.dma_start(mix[q][:, t * NG:(t + 1) * NG, :],
                                                 a.u[bass.ds(pair, 1), :, (4 * q + t) * P:(4 * q + t + 1) * P, :]
                                                 .rearrange("h g p c -> p (h g) c")).then_inc(s_mix[q], 16)
                        if g == 1 and not first:
                            row = column(sp, (hp - 1) * P)
                            sp.wait_ge(s_oz, 2 * hp)
                            sp.dma_start(a.oz[bass.ds(row, P), :], siluz[:]).then_inc(s_ozst, 16)

                load(0, 0)
                load(0, 1)
                load(0, 2)
                bodies(sp, body)
                sp.wait_ge(s_ozst, 16 * HPAIRS)

            @block.gpsimd
            def _(pool):
                def rotate(hp, g, s):
                    n = NT * (NG * hp + g) + s
                    pool.wait_ge(s_turn, n + 1)
                    wait(pool, s_qkt, n - 1)
                    src = turned[s % 2][:].rearrange("p w (h x i) -> p w h x i", x=2, i=HD // 2)
                    dst = rotated[s % 2][:].rearrange("p (h x i) -> p h x i", x=2, i=HD // 2)
                    pool.tensor_tensor(dst[:, :, 0, :], src[:, 1, :, 0, :], src[:, 0, :, 1, :], ALU.subtract).then_inc(s_rot1, 1)
                    pool.tensor_tensor(dst[:, :, 1, :], src[:, 1, :, 1, :], src[:, 0, :, 0, :], ALU.add).then_inc(s_rot, 1)

                def mixture(hp, q):
                    k = 2 * hp + q
                    pool.wait_ge(s_mcoef, k + 1)
                    u = mix[q][:, :, 0:2 * HD].rearrange("p n (e d) -> p n e d", e=2)
                    c = msw[:].rearrange("p t g e -> p (t g) e").unsqueeze(3).broadcast_to([P, 4 * NG, 2, HD])
                    pool.tensor_tensor(u, u, c, ALU.mult).then_inc(s_mm, 1)
                    pool.wait_ge(s_mm, k + 1)
                    ug = mix[q][:].rearrange("p (t g) c -> p t g c", g=NG)
                    pool.tensor_tensor(ug[:, :, 0, 0:P], ug[:, :, 0, 0:P], ug[:, :, 1, 0:P], ALU.add).then_inc(s_ma, 1)
                    pool.wait_ge(s_ma, k + 1)
                    pool.tensor_tensor(ug[:, :, 0, 0:P], ug[:, :, 0, 0:P], ug[:, :, 2, 0:P], ALU.add).then_inc(s_mo, 1)

                def body(hp, first=False, last=False, after=False):
                    for g in range(NG if not after else 2):
                        for s in range(NT):
                            if not after:
                                rotate(hp, g, s)
                            if g == 1 and not first and s in (3, 6):
                                mixture(hp - 1, s // 6)

                bodies(pool, body)

            @block.tensor
            def _(pe):
                def project_qk(hp, g, s):
                    n = NT * (NG * hp + g) + s
                    if s >= 2:
                        pe.wait_ge(s_turn, n - 1)
                    elif g > 0:
                        pe.wait_ge(s_vT, 2 * (NG * hp + g - 1) + s + 1)
                    else:
                        wait(pe, s_z, 2 * (hp - 1) + s + 1)
                    if s == 0:
                        pe.wait_ge(s_wlo, NCH * hp + 3 * g + 2)
                    for k in range(KC):
                        last = three_passes(pe, bank_p[s % 2][:, 0:2 * P], h_hi[:, k, s * P:(s + 1) * P], h_lo[:, k, s * P:(s + 1) * P],
                                            wqk[0][:, k, :], wqk[1][:, k, :], first=k == 0, last=k == KC - 1)
                    last.then_inc(s_qkp, 1)

                def transpose_qk(hp, g, s):
                    n = NT * (NG * hp + g) + s
                    pe.wait_ge(s_rot, n + 1)
                    wait(pe, s_qklo, n)
                    for x in range(2):
                        last = pe.transpose(bank_qk[:, x * P:(x + 1) * P], rotated[s % 2][:, x * P:(x + 1) * P], keep.ident[:])
                    last.then_inc(s_qkt, 1)

                def project_v(hp, g, half, z=False):
                    V = 4 * hp + (3 if z else g)
                    if z:
                        pe.wait_ge(s_vT, 2 * (NG * hp + 2) + half + 1)
                        pe.wait_ge(s_wlo, NCH * hp + 10)
                    else:
                        pe.wait_ge(s_turn, NT * (NG * hp + g) + 7 + half)
                        pe.wait_ge(s_wlo, NCH * hp + 3 * g + 3)
                    slot = wv[(3 if z else g) % 2]
                    for k in range(KC):
                        last = three_passes(pe, bank_p[half][:], slot[0][:, k, :], slot[1][:, k, :],
                                            h_hi[:, k, half * HALF:(half + 1) * HALF], h_lo[:, k, half * HALF:(half + 1) * HALF],
                                            first=k == 0, last=k == KC - 1)
                    last.then_inc(s_zp if z else s_vp, 1)

                def unit_before(hp, g):
                    return (hp - 1, 2) if g == 0 else (hp, g - 1)

                def transpose_v(hp, g, q):
                    A = NG * hp + g
                    if q == 0:
                        pe.wait_ge(s_vT, 2 * A + 2)
                        if g == 1:
                            wait(pe, s_oz, 2 * hp)
                    wait(pe, s_vlo, 2 * A + q)
                    for b in range(4):
                        c = (4 * q + b) * P
                        last = pe.transpose(bank_vo[:, b * P:(b + 1) * P], vT[:, c:c + P], keep.ident[:])
                    last.then_inc(s_vt, 1)

                def scores(hp, g, b):
                    A = NG * hp + g
                    n = NT * A + b
                    if b == 0:
                        pe.wait_ge(s_qklo, NT * A + NT)
                    wait(pe, s_mask, n)
                    j0 = prev_blocks(g, b)[0]
                    for e in range(2):
                        row = slice(e * HD, (e + 1) * HD)
                        q_ = [w[row, 0, b * P:(b + 1) * P] for w in qk[g]]
                        k_ = [w[row, 1, (b - 1 + j0) * P:(b + 1) * P] for w in qk[g]]
                        last = three_passes(pe, bank_s[:, e * HALF + j0 * P:e * HALF + 2 * P], q_[0], q_[1], k_[0], k_[1])
                    last.then_inc(s_sc, 1)

                def transpose_prob(hp, g, b):
                    n = NT * (NG * hp + g) + b
                    pe.wait_ge(s_exp, n + 1)
                    wait(pe, s_ptlo, n)
                    for e in range(2):
                        for j in prev_blocks(g, b):
                            last = pe.transpose(bank_pt[:, (2 * e + j) * P:(2 * e + j + 1) * P], prob[b % 2][:, e, j * P:(j + 1) * P], keep.ident[:])
                    last.then_inc(s_ptr, 1)

                def times_v(hp, g, b):
                    A = NG * hp + g
                    n = NT * A + b
                    if b % 4 == 0:
                        pe.wait_ge(s_vlo, 2 * A + b // 4 + 1)
                    pe.wait_ge(s_ptlo, n + 1)
                    wait(pe, s_u, n)
                    js = prev_blocks(g, b)
                    for e in range(2):
                        col = slice(e * HD, (e + 1) * HD)
                        for j in js:
                            last = three_passes(pe, bank_o[:, col], probT[b % 2][0][:, 2 * e + j, :], probT[b % 2][1][:, 2 * e + j, :],
                                                v[0][:, b - 1 + j, col], v[1][:, b - 1 + j, col], first=j == js[0], last=j == 1)
                    last.then_inc(s_pv, 1)

                def transpose_mixed(hp, q):
                    pe.wait_ge(s_mo, 2 * hp + q + 1)
                    if q == 0:
                        all_v = isinstance(hp, int) and hp == HPAIRS - 1
                        pe.wait_ge(s_vlo, 2 * NG * HPAIRS if all_v else 2 * NG * (hp + 1) + 2)
                    else:
                        pe.wait_ge(s_oz, 2 * hp + 1)
                    for t in range(4):
                        last = pe.transpose(bank_vo[:, t * P:(t + 1) * P], mix[q][:, t * NG, 0:P], keep.ident[:])
                    last.then_inc(s_ot, 1)

                def body(hp, first=False, last=False, after=False):
                    proj = not after
                    for g in range(NG if proj else 2):
                        att = not (first and g == 0) and not (after and g > 0)
                        ah, ag = unit_before(hp, g)
                        for s in range(NT):
                            if proj:
                                project_qk(hp, g, s)
                                if s:
                                    transpose_qk(hp, g, s - 1)
                            if att:
                                if s < 2:
                                    transpose_v(ah, ag, s)
                                scores(ah, ag, s)
                                if s >= 1:
                                    transpose_prob(ah, ag, s - 1)
                                if s >= 2:
                                    times_v(ah, ag, s - 2)
                        if att:
                            transpose_prob(ah, ag, NT - 1)
                        if proj:
                            project_v(hp, g, 0)
                            transpose_qk(hp, g, NT - 1)
                        if att:
                            times_v(ah, ag, NT - 2)
                        if proj:
                            project_v(hp, g, 1)
                        if att:
                            times_v(ah, ag, NT - 1)
                        if g == 1 and not first:
                            transpose_mixed(hp - 1, 0)
                            transpose_mixed(hp - 1, 1)
                        if g == 2:
                            project_v(hp, g, 0, z=True)
                            project_v(hp, g, 1, z=True)

                pe.wait_ge(s_wlo, 2)
                bodies(pe, body)

            @block.scalar
            def _(act):
                def split(hp, j):
                    if j >= NCH:
                        hp, j = hp + 1, j - NCH
                    act.wait_ge(s_raw[j % 2], 16 * (5 * hp + j // 2 + 1))
                    if j in (2, 5, 8, 9):
                        if j == 9:
                            act.wait_ge(s_vp, 6 * hp + 4)
                        elif j == 5:
                            wait(act, s_zp, 2 * hp)
                        else:
                            wait(act, s_vp, 6 * hp + (0 if j == 2 else 2))
                    else:
                        wait(act, s_qkp, NT * (NG * hp + j // 3))
                    dst, c = PLACE[j]
                    act.activation(dst[0][:, :, c:c + P], raw[j % 2][:], ACT.Copy).then_inc(s_whi, 1)

                def qk_hi(hp, g, s):
                    n = NT * (NG * hp + g) + s
                    act.wait_ge(s_qkt, n + 1)
                    act.activation(perm3(qk[g][0][:], g, s * P, P),
                                   bank_qk[:, 0:2 * P].rearrange("p (x m r) -> p x m r", x=2, r=DILATION[g]), ACT.Copy).then_inc(s_qkhi, 1)

                def v_copy(hp, g, half):
                    U = NG * hp + g
                    act.wait_ge(s_vp, 2 * U + half + 1)
                    wait(act, s_vt, 2 * U)
                    act.activation(perm2(vT[:], g, half * HALF, HALF),
                                   bank_p[half][:].rearrange("p (m r) -> p m r", r=DILATION[g]), ACT.Copy).then_inc(s_vT, 1)

                def v_hi(hp, g, q):
                    act.wait_ge(s_vt, 2 * (NG * hp + g) + q + 1)
                    act.activation(v[0][:, 4 * q:4 * q + 4, :], bank_vo[:].rearrange("p (b n) -> p b n", b=4), ACT.Copy).then_inc(s_vhi, 1)

                def z_exp(hp, half):
                    act.wait_ge(s_zp, 2 * hp + half + 1)
                    wait(act, s_ozst, 16 * hp)
                    act.activation(siluz[:, half * HALF:(half + 1) * HALF], bank_p[half][:], ACT.Exp, scale=-1.0).then_inc(s_ez, 1)

                def exps(hp, g, b):
                    n = NT * (NG * hp + g) + b
                    act.wait_ge(s_bias, n + 1)
                    j0 = prev_blocks(g, b)[0]
                    for e in range(2):
                        row = prob[b % 2][:, e, j0 * P:2 * P]
                        last = act.activation(row, row, ACT.Exp, bias=bias[b % 2][:, e:e + 1], scale=SCALE,
                                              accum_out=urow[b % 4][:, 2 * HD + 2 + e:2 * HD + 3 + e])
                    last.then_inc(s_exp, 1)

                def probT_hi(hp, g, b):
                    n = NT * (NG * hp + g) + b
                    act.wait_ge(s_ptr, n + 1)
                    wait(act, s_pv, n - 1)
                    j0 = prev_blocks(g, b)[0]
                    act.activation(probT[b % 2][0][:].rearrange("p (e j) n -> p e j n", e=2)[:, :, j0:2, :],
                                   bank_pt[:].rearrange("p (e j n) -> p e j n", e=2, j=2)[:, :, j0:2, :], ACT.Copy).then_inc(s_pthi, 1)

                def u_copy(hp, g, b):
                    n = NT * (NG * hp + g) + b
                    act.wait_ge(s_pv, n + 1)
                    act.activation(urow[b % 4][:, 0:2 * HD], bank_o[:, 0:2 * HD], ACT.Copy).then_inc(s_u, 1)

                def mix_exp(hp, q):
                    act.wait_ge(s_md, 2 * hp + q + 1)
                    act.activation(mw[:], mw[:], ACT.Exp, scale=SCALE).then_inc(s_mw, 1)

                def unit_before(hp, g):
                    return (hp - 1, 2) if g == 0 else (hp, g - 1)

                def body(hp, first=False, last=False, after=False):
                    proj = not after
                    for g in range(NG if proj else 2):
                        att = not (first and g == 0) and not (after and g > 0)
                        ah, ag = unit_before(hp, g)
                        for s in range(NT):
                            if proj and s:
                                qk_hi(hp, g, s - 1)
                            if att:
                                if s < 2:
                                    v_hi(ah, ag, s)
                                exps(ah, ag, s)
                                if s >= 1:
                                    probT_hi(ah, ag, s - 1)
                                if s >= 2:
                                    u_copy(ah, ag, s - 2)
                            if g == 1 and not first and s in (2, 5):
                                mix_exp(hp - 1, s // 5)
                            if proj and s == 3:
                                split(hp, 3 * g + 2)
                            if g == 2 and s == 5:
                                split(hp, 9)
                        if att:
                            probT_hi(ah, ag, NT - 1)
                        if proj:
                            if g < 2:
                                split(hp, 3 * g + 3)
                                split(hp, 3 * g + 4)
                            elif not last:
                                split(hp, 10)
                                split(hp, 11)
                            v_copy(hp, g, 0)
                            qk_hi(hp, g, NT - 1)
                        if att:
                            u_copy(ah, ag, NT - 2)
                        if proj:
                            v_copy(hp, g, 1)
                        if att:
                            u_copy(ah, ag, NT - 1)
                        if g == 2:
                            z_exp(hp, 0)
                            z_exp(hp, 1)

                split(0, 0)
                split(0, 1)
                bodies(act, body)

            @block.vector
            def _(dve):
                def split(hp, j):
                    if j >= NCH:
                        hp, j = hp + 1, j - NCH
                    dve.wait_ge(s_whi, NCH * hp + j + 1)
                    dst, c = PLACE[j]
                    dve.tensor_tensor(dst[1][:, :, c:c + P], raw[j % 2][:], f(dst[0][:, :, c:c + P]), ALU.subtract).then_inc(s_wlo, 1)

                def turn(hp, g, s):
                    n = NT * (NG * hp + g) + s
                    dve.wait_ge(s_qkp, n + 1)
                    wait(dve, s_rot, n - 1)
                    for q in range(2):
                        table = keep.rope[:, q, s, :].unsqueeze(1).broadcast_to([P, 8, HD // 2])
                        last = dve.tensor_tensor(turned[s % 2][:, q, :].rearrange("p (n i) -> p n i", i=HD // 2),
                                                 bank_p[s % 2][:, 0:2 * P].rearrange("p (n i) -> p n i", i=HD // 2), table, ALU.mult)
                    last.then_inc(s_turn, 1)

                def qk_lo(hp, g, s):
                    n = NT * (NG * hp + g) + s
                    dve.wait_ge(s_qkhi, n + 1)
                    dve.tensor_tensor(perm3(qk[g][1][:], g, s * P, P),
                                      bank_qk[:, 0:2 * P].rearrange("p (x m r) -> p x m r", x=2, r=DILATION[g]),
                                      perm3(f(qk[g][0][:]), g, s * P, P), ALU.subtract).then_inc(s_qklo, 1)

                def v_lo(hp, g, q):
                    dve.wait_ge(s_vhi, 2 * (NG * hp + g) + q + 1)
                    dve.tensor_tensor(v[1][:, 4 * q:4 * q + 4, :], bank_vo[:].rearrange("p (b n) -> p b n", b=4),
                                      f(v[0][:, 4 * q:4 * q + 4, :]), ALU.subtract).then_inc(s_vlo, 1)

                def z_silu(hp, half):
                    n = 2 * (2 * hp + half)
                    dve.wait_ge(s_ez, 2 * hp + half + 1)
                    zs = siluz[:, half * HALF:(half + 1) * HALF]
                    dve.tensor_scalar(zs, zs, 1.0, None, ALU.add).then_inc(s_zchain, 1)
                    dve.wait_ge(s_zchain, n + 1)
                    dve.reciprocal(zs, zs).then_inc(s_zchain, 1)
                    dve.wait_ge(s_zchain, n + 2)
                    dve.tensor_tensor(zs, bank_p[half][:], zs, ALU.mult).then_inc(s_z, 1)

                def mask_and_max(hp, g, b):
                    A = NG * hp + g
                    n = NT * A + b
                    dve.wait_ge(s_sc, n + 1)
                    wait(dve, s_ptr, n - 1)
                    wait(dve, s_ust[b % 4], 16 * (2 * A + b // 4))
                    j0 = prev_blocks(g, b)[0]
                    if g == 2:
                        mask = keep.diag[:].unsqueeze(1).broadcast_to([P, 2, P])
                    else:
                        mask = keep.band[:, j0 * P:2 * P].unsqueeze(1).broadcast_to([P, 2, (2 - j0) * P])
                    dst = prob[b % 2][:, :, j0 * P:2 * P]
                    dve.tensor_tensor(dst, bank_s[:].rearrange("p (e j) -> p e j", e=2)[:, :, j0 * P:2 * P], mask, ALU.add).then_inc(s_mask, 1)
                    dve.wait_ge(s_mask, n + 1)
                    top = urow[b % 4][:, 2 * HD:2 * HD + 2]
                    dve.reduce_max(top, dst, axis=AXX).then_inc(s_max, 1)
                    dve.wait_ge(s_max, n + 1)
                    dve.tensor_scalar(bias[b % 2][:], top, -SCALE, None, ALU.mult).then_inc(s_bias, 1)

                def probT_lo(hp, g, b):
                    n = NT * (NG * hp + g) + b
                    dve.wait_ge(s_pthi, n + 1)
                    j0 = prev_blocks(g, b)[0]
                    hi, lo = (w[:].rearrange("p (e j) n -> p e j n", e=2)[:, :, j0:2, :] for w in probT[b % 2])
                    dve.tensor_tensor(lo, bank_pt[:].rearrange("p (e j n) -> p e j n", e=2, j=2)[:, :, j0:2, :], f(hi), ALU.subtract).then_inc(s_ptlo, 1)

                def mix_difference(hp, q):
                    k = 2 * hp + q
                    dve.wait_ge(s_mix[q], 64 * (hp + 1))
                    mg = mix[q][:, :, 2 * HD:2 * HD + 2].rearrange("p (t g) e -> p t g e", g=NG)
                    dve.tensor_tensor(mmax[:], mg[:, :, 0, :], mg[:, :, 1, :], ALU.max).then_inc(s_mc, 1)
                    dve.wait_ge(s_mc, 6 * k + 1)
                    dve.tensor_tensor(mmax[:], mmax[:], mg[:, :, 2, :], ALU.max).then_inc(s_mc, 1)
                    dve.wait_ge(s_mc, 6 * k + 2)
                    dve.tensor_tensor(mw[:], mg, mmax[:].unsqueeze(2).broadcast_to([P, 4, NG, 2]), ALU.subtract).then_inc(s_md, 1)

                def mix_coefficients(hp, q):
                    k = 2 * hp + q
                    dve.wait_ge(s_mw, k + 1)
                    wait(dve, s_mm, k)
                    sg = mix[q][:, :, 2 * HD + 2:2 * HD + 4].rearrange("p (t g) e -> p t g e", g=NG)
                    dve.tensor_tensor(msw[:], mw[:], sg, ALU.mult).then_inc(s_mc, 1)
                    dve.wait_ge(s_mc, 6 * k + 3)
                    dve.tensor_tensor(mden[:], msw[:, :, 0, :], msw[:, :, 1, :], ALU.add).then_inc(s_mc, 1)
                    dve.wait_ge(s_mc, 6 * k + 4)
                    dve.tensor_tensor(mden[:], mden[:], msw[:, :, 2, :], ALU.add).then_inc(s_mc, 1)
                    dve.wait_ge(s_mc, 6 * k + 5)
                    dve.reciprocal(mden[:], mden[:]).then_inc(s_mc, 1)
                    dve.wait_ge(s_mc, 6 * k + 6)
                    dve.tensor_tensor(msw[:], mw[:], mden[:].unsqueeze(2).broadcast_to([P, 4, NG, 2]), ALU.mult).then_inc(s_mcoef, 1)

                def gate(hp, q):
                    dve.wait_ge(s_ot, 2 * hp + q + 1)
                    c = slice(q * HALF, (q + 1) * HALF)
                    dve.tensor_tensor(siluz[:, c], bank_vo[:], siluz[:, c], ALU.mult).then_inc(s_oz, 1)

                def unit_before(hp, g):
                    return (hp - 1, 2) if g == 0 else (hp, g - 1)

                def body(hp, first=False, last=False, after=False):
                    proj = not after
                    for g in range(NG if proj else 2):
                        att = not (first and g == 0) and not (after and g > 0)
                        ah, ag = unit_before(hp, g)
                        for s in range(NT):
                            if proj:
                                turn(hp, g, s)
                                if s:
                                    qk_lo(hp, g, s - 1)
                            if att:
                                if s < 2:
                                    v_lo(ah, ag, s)
                                mask_and_max(ah, ag, s)
                                if s >= 1:
                                    probT_lo(ah, ag, s - 1)
                            if g == 1 and not first:
                                if s in (2, 5):
                                    mix_difference(hp - 1, s // 5)
                                if s in (3, 6):
                                    mix_coefficients(hp - 1, s // 6)
                            if proj and s == 3:
                                split(hp, 3 * g + 2)
                            if g == 2 and s == 5:
                                split(hp, 9)
                        if att:
                            probT_lo(ah, ag, NT - 1)
                        if proj:
                            if g < 2:
                                split(hp, 3 * g + 3)
                                split(hp, 3 * g + 4)
                            elif not last:
                                split(hp, 10)
                                split(hp, 11)
                            qk_lo(hp, g, NT - 1)
                        if g == 1 and not first:
                            gate(hp - 1, 0)
                            gate(hp - 1, 1)
                        if g == 2:
                            z_silu(hp, 0)
                            z_silu(hp, 1)

                split(0, 0)
                split(0, 1)
                bodies(dve, body)
        m.clear()

def tail(nc, a, keep, l):
    h_hi, h_lo = keep.h
    x = keep.x
    w_out = (a.attn_w_out if l == 0 else a.conv_w_out)[0].rearrange("(k p) c -> p k c", p=P)
    w_gate = a.ple_w_gate[l].rearrange("(k p) c -> p k c", p=P)
    with ExitStack() as ctx:
        m = Memory(nc, ctx, f"t{l}")
        raw = [m.sb(f"raw{i}", [P, 2, HALF]) for i in range(2)]
        w = [[m.sb(f"w{i}_{n}", [P, KC, HALF], F32R) for n in ("hi", "lo")] for i in range(2)]
        y0 = m.sb("y0", [P, NT, HALF])
        gain = m.sb("gain", [P, DM])
        scratch = m.sb("scratch", [P, HALF])
        ssq = m.sb("ssq", [P, 2, NT])
        rstd = m.sb("rstd", [P, NT])
        part = [m.sb(f"part{i}", [P, HALF]) for i in range(2)]
        pp = [m.sb(f"pp{i}", [P, HALF]) for i in range(2)]
        gated = [m.sb(f"gated{i}", [P, HALF]) for i in range(2)]
        bank_y = [m.ps(f"bank_y{i}") for i in range(4)]
        bank_t = [m.ps(f"bank_t{i}") for i in range(2)]

        s_gain = m.sem("gain_in")
        s_x = m.sem("x_in")
        s_raw = [m.sem(f"raw_in{i}") for i in range(2)]
        s_oz = [m.sem(f"act_in{i}") for i in range(2)]
        s_ahi = m.sem("act_hi_done")
        s_alo = m.sem("act_lo_done")
        s_whi = m.sem("w_hi_done")
        s_wlo = m.sem("w_lo_done")
        s_y = m.sem("tile_multiplied")
        s_free = m.sem("y0_bank_read")
        s_sq = m.sem("ssq_done")
        s_var = m.sem("var_chain")
        s_rstd = m.sem("rstd_done")
        s_part = m.sem("update_ready")
        s_yread = m.sem("y1_bank_read")
        s_x1 = m.sem("x_updated")
        s_xt = m.sem("x_transposed")
        s_xhi = m.sem("x_hi_done")
        s_xlo = m.sem("x_lo_done")
        s_pp = [m.sem(f"pp_in{i}") for i in range(2)]
        s_sig = m.sem("sigmoid_done")
        s_gated = m.sem("gated")
        s_x2 = m.sem("x_final")
        s_out = m.sem("out_stored")

        with nc.Block() as block:
            @block.sync
            def _(sp):
                if l == 0:
                    for c in range(KC):
                        if c >= 2:
                            sp.wait_ge(s_alo, c - 1)
                        sp.dma_start(y0[:, 2 * (c % 2):2 * (c % 2) + 2, :].rearrange("p a n -> p (a n)"),
                                     a.oz[c * P:(c + 1) * P, :]).then_inc(s_oz[c % 2], 16)
                        if c == 0:
                            sp.dma_start(x[:], a.x[0].rearrange("(t p) c -> p t c", p=P)).then_inc(s_x, 16)
                sp.dma_start(gain[:], a.post_norm_g[l, :].partition_broadcast(P)).then_inc(s_gain, 16)

                def product(n):
                    half, t = n // NT, n % NT
                    if n >= 2:
                        sp.wait_ge(s_gated, n - 1)
                    sp.dma_start(pp[n % 2][:], a.pp[l, t * P:(t + 1) * P, half * HALF:(half + 1) * HALF]).then_inc(s_pp[n % 2], 16)

                product(0)
                product(1)
                for n in range(2 * NT):
                    if n >= 2:
                        product(n)
                    if l == 1 and n >= NT:
                        t = n - NT
                        sp.wait_ge(s_x2, n + 1)
                        sp.dma_start(a.out[0, t * P:(t + 1) * P, :], x[:, t, :]).then_inc(s_out, 16)
                if l == 1:
                    sp.wait_ge(s_out, 16 * NT)

            @block.gpsimd
            def _(pool):
                def load(n):
                    j, c = n // 4, n % 4
                    if n >= 2:
                        pool.wait_ge(s_wlo, n - 1)
                    src = (w_out if j < 2 else w_gate)[:, 2 * c:2 * c + 2, (j % 2) * HALF:(j % 2 + 1) * HALF]
                    pool.dma_start(raw[n % 2][:], src).then_inc(s_raw[n % 2], 16)

                for n in range(10):
                    load(n)
                for t in range(NT):
                    c = slice(t, t + 1)
                    pool.wait_ge(s_sq, t + 1)
                    pool.tensor_tensor(rstd[:, c], ssq[:, 0, c], ssq[:, 1, c], ALU.add).then_inc(s_var, 1)
                    pool.wait_ge(s_var, 2 * t + 1)
                    pool.tensor_scalar(rstd[:, c], rstd[:, c], 1.0 / DM, RMS_EPS, ALU.mult, ALU.add).then_inc(s_var, 1)
                    pool.wait_ge(s_var, 2 * t + 2)
                    pool.tensor_tensor(rstd[:, c], rstd[:, c], keep.minus_half[:, 0:1], ALU.pow).then_inc(s_rstd, 1)
                    if t % 2 == 0:
                        load(10 + t // 2)
                for n in range(14, 16):
                    load(n)

            @block.tensor
            def _(pe):
                def product(j, t):
                    n = NT * j + t
                    if n >= 4:
                        if n - 4 < NT:
                            pe.wait_ge(s_free, n - 3)
                        elif n - 4 < 2 * NT:
                            pe.wait_ge(s_yread, n - 4 - NT + 1)
                        else:
                            pe.wait_ge(s_sig, n - 4 - 2 * NT + 1)
                    if t == 0:
                        pe.wait_ge(s_wlo, 4 * j + 4)
                    if j == 0 and t == 0 and l == 0:
                        pe.wait_ge(s_alo, KC)
                    if j == 2:
                        pe.wait_ge(s_xlo, 2 * t + 2)
                    for k in range(KC):
                        last = three_passes(pe, bank_y[n % 4][:], h_hi[:, k, t * P:(t + 1) * P], h_lo[:, k, t * P:(t + 1) * P],
                                            w[j % 2][0][:, k, :], w[j % 2][1][:, k, :], first=k == 0, last=k == KC - 1)
                    last.then_inc(s_y, 1)

                def transpose_x(t):
                    pe.wait_ge(s_x1, t + 1)
                    for half in range(2):
                        n = 2 * t + half
                        if n >= 2:
                            pe.wait_ge(s_xlo, n - 1)
                        for k in range(4):
                            c = 4 * half + k
                            last = pe.transpose(bank_t[half][:, k * P:(k + 1) * P], x[:, t, c * P:(c + 1) * P], keep.ident[:])
                        last.then_inc(s_xt, 1)

                for t in range(NT):
                    product(0, t)
                for t in range(NT):
                    product(1, t)
                    if t >= 1:
                        transpose_x(t - 1)
                product(2, 0)
                transpose_x(NT - 1)
                for t in range(1, NT):
                    product(2, t)
                for t in range(NT):
                    product(3, t)

            @block.scalar
            def _(act):
                if l == 0:
                    for c in range(KC):
                        act.wait_ge(s_oz[c % 2], 16 * (c // 2 + 1))
                        act.activation(h_hi[:, c, :], y0[:, 2 * (c % 2):2 * (c % 2) + 2, :].rearrange("p a n -> p (a n)"), ACT.Copy).then_inc(s_ahi, 1)

                def split(n):
                    j, c = n // 4, n % 4
                    act.wait_ge(s_raw[n % 2], 16 * (n // 2 + 1))
                    if j >= 2:
                        act.wait_ge(s_y, NT * (j - 1))
                    act.activation(w[j % 2][0][:, 2 * c:2 * c + 2, :], raw[n % 2][:], ACT.Copy).then_inc(s_whi, 1)

                def x_hi(t):
                    for half in range(2):
                        act.wait_ge(s_xt, 2 * t + half + 1)
                        act.activation(h_hi[:, 4 * half:4 * half + 4, t * P:(t + 1) * P],
                                       bank_t[half][:].rearrange("p (k n) -> p k n", k=4), ACT.Copy).then_inc(s_xhi, 1)

                for n in range(4):
                    split(n)
                if l == 0:
                    act.wait_ge(s_alo, KC)
                for t in range(NT):
                    if t % 2 == 0:
                        split(4 + t // 2)
                    act.wait_ge(s_y, t + 1)
                    act.activation(y0[:, t, :], bank_y[t % 4][:], ACT.Copy)
                    wait(act, s_free, t)
                    act.activation(scratch[:], bank_y[t % 4][:], ACT.Square, accum_out=ssq[:, 0, t:t + 1]).then_inc(s_free, 1)
                for t in range(NT):
                    if t % 2 == 0:
                        split(8 + t // 2)
                    act.wait_ge(s_y, NT + t + 1)
                    act.wait_ge(*((s_sq, t) if t else (s_free, NT)))
                    act.activation(scratch[:], bank_y[t % 4][:], ACT.Square, accum_out=ssq[:, 1, t:t + 1]).then_inc(s_sq, 1)
                    if t >= 1:
                        x_hi(t - 1)
                x_hi(NT - 1)
                for n in range(2 * NT):
                    if n < NT and n % 2 == 0:
                        split(12 + n // 2)
                    act.wait_ge(s_y, 2 * NT + n + 1)
                    if n >= 2:
                        act.wait_ge(s_x2, n - 1)
                    act.activation(gated[n % 2][:], bank_y[n % 4][:], ACT.Sigmoid).then_inc(s_sig, 1)

            @block.vector
            def _(dve):
                if l == 0:
                    for c in range(KC):
                        dve.wait_ge(s_ahi, c + 1)
                        dve.tensor_tensor(h_lo[:, c, :], y0[:, 2 * (c % 2):2 * (c % 2) + 2, :].rearrange("p a n -> p (a n)"), f(h_hi[:, c, :]),
                                          ALU.subtract).then_inc(s_alo, 1)

                def split(n):
                    j, c = n // 4, n % 4
                    dve.wait_ge(s_whi, n + 1)
                    dve.tensor_tensor(w[j % 2][1][:, 2 * c:2 * c + 2, :], raw[n % 2][:], f(w[j % 2][0][:, 2 * c:2 * c + 2, :]),
                                      ALU.subtract).then_inc(s_wlo, 1)

                def x_lo(t):
                    for half in range(2):
                        dve.wait_ge(s_xhi, 2 * t + half + 1)
                        sl = (slice(None), slice(4 * half, 4 * half + 4), slice(t * P, (t + 1) * P))
                        dve.tensor_tensor(h_lo[sl], bank_t[half][:].rearrange("p (k n) -> p k n", k=4), f(h_hi[sl]), ALU.subtract).then_inc(s_xlo, 1)

                for n in range(4):
                    split(n)
                for c in range(4):
                    split(4 + c)
                dve.wait_ge(s_gain, 16)
                if l == 0:
                    dve.wait_ge(s_x, 16)
                for t in range(NT):
                    if t % 2 == 0:
                        split(8 + t // 2)
                    dve.wait_ge(s_rstd, t + 1)
                    wait(dve, s_x1, t)
                    r = rstd[:, t:t + 1]
                    dve.scalar_tensor_tensor(part[1][:], bank_y[t % 4][:], r, gain[:, HALF:DM], ALU.mult, ALU.mult).then_inc(s_yread, 1)
                    dve.scalar_tensor_tensor(part[0][:], y0[:, t, :], r, gain[:, 0:HALF], ALU.mult, ALU.mult).then_inc(s_part, 1)
                    dve.wait_ge(s_yread, t + 1)
                    dve.tensor_tensor(x[:, t, HALF:DM], x[:, t, HALF:DM], part[1][:], ALU.add)
                    dve.wait_ge(s_part, t + 1)
                    dve.tensor_tensor(x[:, t, 0:HALF], x[:, t, 0:HALF], part[0][:], ALU.add).then_inc(s_x1, 1)
                    if t >= 1:
                        x_lo(t - 1)
                x_lo(NT - 1)
                for n in range(2 * NT):
                    if n < NT and n % 2 == 0:
                        split(12 + n // 2)
                    half, t = n // NT, n % NT
                    dve.wait_ge(s_sig, n + 1)
                    dve.wait_ge(s_pp[n % 2], 16 * (n // 2 + 1))
                    dve.tensor_tensor(gated[n % 2][:], gated[n % 2][:], pp[n % 2][:], ALU.mult).then_inc(s_gated, 1)
                    dve.wait_ge(s_gated, n + 1)
                    c = slice(half * HALF, (half + 1) * HALF)
                    dve.tensor_tensor(x[:, t, c], x[:, t, c], gated[n % 2][:], ALU.add).then_inc(s_x2, 1)
        if l == 0:
            m.clear()


def conv_norm(nc, a, keep):
    with ExitStack() as ctx:
        m = Memory(nc, ctx, "cn")
        gain = m.sb("gain", [P, DM])
        rows = m.sb("rows", [TAPS + 3, DM])
        banks = [m.ps(f"bank{i}") for i in range(2)]
        bank_c = m.ps("bank_c")
        s_gain = m.sem("gain_in")
        s_rows = m.sem("rows_in")
        s_ct = m.sem("rows_transposed")
        s_chan = m.sem("channels_done")
        pn = PreNorm(m, keep.x, gain, keep.h, banks, keep.ident, keep.minus_half[:, 0:1])
        with nc.Block() as block:
            @block.sync
            def _(sp):
                sp.dma_start(gain[:], a.pre_norm_g[1, :].partition_broadcast(P)).then_inc(s_gain, 16)
                sp.dma_start(rows[0:TAPS, :], a.conv_dw_w[0]).then_inc(s_rows, 16)
                for i, r in enumerate((a.conv_dw_b, a.conv_ln_g, a.conv_ln_b)):
                    sp.dma_start(rows[TAPS + i:TAPS + i + 1, :], r[0:1, :]).then_inc(s_rows, 16)

            @block.gpsimd
            def _(pool):
                for t in range(NT):
                    pn.pool_rstd(pool, t)

            @block.scalar
            def _(act):
                for t in range(NT):
                    pn.act_squares(act, t)
                    if t >= 2:
                        pn.act_hi(act, t - 2)
                for t in range(NT - 2, NT):
                    pn.act_hi(act, t)

            @block.vector
            def _(dve):
                dve.wait_ge(s_ct, 1)
                dve.tensor_copy(keep.chan[:].rearrange("p c n -> p (c n)"), bank_c[:, 0:KC * (TAPS + 3)]).then_inc(s_chan, 1)
                dve.wait_ge(s_gain, 16)
                for t in range(NT):
                    pn.dve_scale(dve, t)
                    if t >= 1:
                        pn.dve_lo(dve, t - 1)
                pn.dve_lo(dve, NT - 1)

            @block.tensor
            def _(pe):
                n = TAPS + 3
                pe.wait_ge(s_rows, 64)
                for c in range(KC):
                    last = pe.transpose(bank_c[:, c * n:(c + 1) * n], rows[:, c * P:(c + 1) * P], keep.ident[0:n, 0:n])
                last.then_inc(s_ct, 1)
                for t in range(NT):
                    pn.pe_transposes(pe, t)
        m.clear()


ACT_TAPS = tuple(range(14))
DVE_TAPS = tuple(range(14, TAPS))


def conv(nc, a, keep):
    h_hi, h_lo = keep.h
    PAD = TAPS - 1
    w_in = a.conv_w_in[0].rearrange("(k p) c -> p k c", p=P)
    with ExitStack() as ctx:
        m = Memory(nc, ctx, "cv")
        raw = [m.sb(f"raw{i}", [P, KC, P]) for i in range(2)]
        w = [[m.sb(f"w{i}_{n}", [P, KC, P], F32R) for n in ("hi", "lo")] for i in range(2)]
        cv = m.sb("cv", [P, KC, SEQ])
        u = [m.sb(f"u{i}", [P, PAD + SEQ]) for i in range(2)]
        sig = [m.sb(f"sig{i}", [P, HALF]) for i in range(2)]
        tap = [m.sb(f"tap{i}", [P, SEQ]) for i in range(2)]
        acc = [m.sb(f"acc{i}", [P, SEQ]) for i in range(2)]
        dacc = [m.sb(f"dacc{i}", [P, SEQ]) for i in range(2)]
        total = m.sb("total", [P, SEQ])
        cw = [m.sb(f"cw{i}", [P, TAPS + 3]) for i in range(2)]
        mean_of = m.sb("mean_of", [P, P])
        banks = [m.ps(f"bank{i}") for i in range(8)]

        s_raw = [m.sem(f"raw_in{i}") for i in range(2)]
        s_turn = m.sem("buffer_free")
        s_pad = m.sem("pads_zero")
        s_cw = m.sem("channel_weights")
        s_whi = m.sem("w_hi_done")
        s_wlo = m.sem("w_lo_done")
        s_b = m.sem("b_projected")
        s_a = m.sem("a_projected")
        s_sig = m.sem("sigmoid_done")
        s_u = m.sem("u_done")
        s_dtap = m.sem("dve_taps")
        s_atap = m.sem("act_taps")
        s_acc0 = m.sem("acc_started")
        s_padd = m.sem("pool_adds")
        s_cv = m.sem("conv_done")
        s_tot = m.sem("totals_done")
        NA, ND = len(ACT_TAPS), len(DVE_TAPS)

        def bodies(eng, body):
            body(0)
            with eng.Fori(1, KC // 2) as i:
                body(i)

        with nc.Block() as block:
            @block.sync
            def _(sp):
                def load(c, j):
                    wait(sp, s_wlo, 2 * c + j - 1)
                    sp.sem_inc(s_turn, 1)
                    sp.dma_start(raw[j][:], w_in[:, :, bass.ds(c * P + (DM if j == 0 else 0), P)]).then_inc(s_raw[j], 16)

                def body(i):
                    for q in range(2):
                        for j in range(2):
                            load(2 * i + q, j)

                bodies(sp, body)

            @block.gpsimd
            def _(pool):
                for q in range(2):
                    pool.memset(u[q][:, 0:PAD], 0.0).then_inc(s_pad, 1)
                pool.memset(mean_of[:], 1.0 / DM)
                pool.memset(total[:], 0.0).then_inc(s_tot, 1)

                def body(i):
                    for q in range(2):
                        c = 2 * i + q
                        for k in range(1, NA):
                            if k == 1:
                                pool.wait_ge(s_acc0, c + 1)
                            pool.wait_ge(s_atap, (NA - 1) * c + k)
                            wait(pool, s_padd, (NA - 1) * c + k - 1)
                            pool.tensor_tensor(acc[q][:], acc[q][:], tap[k % 2][:], ALU.add).then_inc(s_padd, 1)
                        pool.wait_ge(s_padd, (NA - 1) * (c + 1))
                        pool.wait_ge(s_tot, 2 * c + 1)
                        pool.tensor_tensor(total[:], total[:], acc[q][:], ALU.add).then_inc(s_tot, 1)
                        pool.wait_ge(s_dtap, ND * (c + 1))
                        pool.wait_ge(s_tot, 2 * c + 2)
                        pool.tensor_tensor(total[:], total[:], dacc[q][:], ALU.add).then_inc(s_tot, 1)

                bodies(pool, body)

            @block.tensor
            def _(pe):
                def project(c, q, j):
                    pe.wait_ge(s_wlo, 2 * c + j + 1)
                    for half in range(2):
                        wait(pe, s_u if j else s_sig, 2 * (c - 2) + half + 1)
                        for k in range(KC):
                            last = three_passes(pe, banks[4 * q + 2 * j + half][:], w[j][0][:, k, :], w[j][1][:, k, :],
                                                h_hi[:, k, half * HALF:(half + 1) * HALF], h_lo[:, k, half * HALF:(half + 1) * HALF],
                                                first=k == 0, last=k == KC - 1)
                        last.then_inc(s_a if j else s_b, 1)

                def body(i):
                    for q in range(2):
                        for j in range(2):
                            project(2 * i + q, q, j)

                bodies(pe, body)

            @block.scalar
            def _(act):
                def split(c, j):
                    act.wait_ge(s_raw[j], 16 * (c + 1))
                    wait(act, s_a if j else s_b, 2 * c)
                    act.activation(w[j][0][:], raw[j][:], ACT.Copy).then_inc(s_whi, 1)

                def body(i, last=False):
                    for q in range(2):
                        c = 2 * i + q
                        for half in range(2):
                            act.wait_ge(s_b, 2 * c + half + 1)
                            wait(act, s_u, 2 * (c - 1) + half + 1)
                            act.activation(sig[half][:], banks[4 * q + half][:], ACT.Sigmoid).then_inc(s_sig, 1)
                        if not (last and q == 1):
                            split(c + 1, 0)
                            split(c + 1, 1)
                        act.wait_ge(s_u, 2 * c + 2)
                        act.wait_ge(s_cw, c + 1)
                        for n, k in enumerate(ACT_TAPS):
                            dst = acc[q] if n == 0 else tap[n % 2]
                            if n == 0:
                                wait(act, s_cv, c - 1)
                                wait(act, s_tot, 2 * (c - 1) + 1)
                            elif n == 1 or n == 2:
                                wait(act, s_padd, (NA - 1) * c)
                            else:
                                act.wait_ge(s_padd, (NA - 1) * c + n - 2)
                            act.activation(dst[:], u[q][:, k:k + SEQ], ACT.Copy, scale=cw[q][:, k:k + 1]).then_inc(s_acc0 if n == 0 else s_atap, 1)

                split(0, 0)
                split(0, 1)
                body(0)
                with act.Fori(1, KC // 2 - 1) as i:
                    body(i)
                body(KC // 2 - 1, last=True)

            @block.vector
            def _(dve):
                def split(c, j):
                    dve.wait_ge(s_whi, 2 * c + j + 1)
                    dve.tensor_tensor(w[j][1][:], raw[j][:], f(w[j][0][:]), ALU.subtract).then_inc(s_wlo, 1)

                def body(i, last=False):
                    for q in range(2):
                        c = 2 * i + q
                        wait(dve, s_atap, (NA - 1) * (c - 1))
                        dve.tensor_copy(cw[q][:], keep.chan[:, bass.ds(c, 1), :].rearrange("p o n -> p (o n)")).then_inc(s_cw, 1)
                        more = not (last and q == 1)
                        if more:
                            split(c + 1, 0)
                        for half in range(2):
                            dve.wait_ge(s_a, 2 * c + half + 1)
                            dve.wait_ge(s_sig, 2 * c + half + 1)
                            dve.tensor_tensor(u[q][:, PAD + half * HALF:PAD + (half + 1) * HALF], banks[4 * q + 2 + half][:], sig[half][:], ALU.mult).then_inc(s_u, 1)
                        if more:
                            split(c + 1, 1)
                        dve.wait_ge(s_u, 2 * c + 2)
                        dve.wait_ge(s_cw, c + 1)
                        wait(dve, s_tot, 2 * (c - 1) + 1)
                        dst = dacc[q][:]
                        for n, k in enumerate(DVE_TAPS):
                            src = u[q][:, k:k + SEQ]
                            if n == 0:
                                dve.tensor_scalar(dst, src, cw[q][:, k:k + 1], cw[q][:, TAPS:TAPS + 1], ALU.mult, ALU.add).then_inc(s_dtap, 1)
                            else:
                                dve.wait_ge(s_dtap, ND * c + n)
                                dve.scalar_tensor_tensor(dst, src, cw[q][:, k:k + 1], dst, ALU.mult, ALU.add).then_inc(s_dtap, 1)
                        dve.wait_ge(s_dtap, ND * (c + 1))
                        dve.wait_ge(s_padd, (NA - 1) * (c + 1))
                        dve.tensor_tensor(cv[:, bass.ds(c, 1), :].rearrange("p o n -> p (o n)"), dst, acc[q][:], ALU.add).then_inc(s_cv, 1)

                split(0, 0)
                split(0, 1)
                dve.wait_ge(s_pad, 2)
                body(0)
                with dve.Fori(1, KC // 2 - 1) as i:
                    body(i)
                body(KC // 2 - 1, last=True)

        zs = [m.sb(f"zs{i}", [P, SEQ]) for i in range(3)]
        n_raw = [m.sem(f"z_raw_in{i}") for i in range(2)]
        n_whi = m.sem("z_w_hi_done")
        n_wlo = m.sem("z_w_lo_done")
        n_z = m.sem("z_projected")
        n_zs = m.sem("z_silu_done")
        n_mean = m.sem("mean_done")
        n_d = m.sem("centred")
        n_sq = m.sem("squared")
        n_sum = m.sem("squares_summed")
        n_var = m.sem("variance_done")
        n_eps = m.sem("variance_eps")
        n_rstd = m.sem("rstd_done")
        n_t = m.sem("normalised")
        n_s = m.sem("ln_silu_done")
        n_g = m.sem("gated")
        n_ghi = m.sem("gated_hi_done")
        n_glo = m.sem("gated_lo_done")
        rstd = acc[0]
        mean_bank = banks[6:8]
        with nc.Block() as block:
            @block.sync
            def _(sp):
                for c in range(KC):
                    if c >= 2:
                        sp.wait_ge(n_wlo, c - 1)
                    sp.dma_start(raw[c % 2][:], w_in[:, :, 2 * DM + c * P:2 * DM + (c + 1) * P]).then_inc(n_raw[c % 2], 16)

            @block.tensor
            def _(pe):
                def moments(src, sem):
                    for half in range(2):
                        last = pe.matmul(mean_bank[half][:], mean_of[:], src[:, half * HALF:(half + 1) * HALF], start=True, stop=True)
                    last.then_inc(sem, 1)

                def project(c):
                    pe.wait_ge(n_wlo, c + 1)
                    for half in range(2):
                        if c >= 3:
                            pe.wait_ge(n_zs, 2 * (c - 3) + half + 1)
                        for k in range(KC):
                            last = three_passes(pe, banks[2 * (c % 3) + half][:], w[c % 2][0][:, k, :], w[c % 2][1][:, k, :],
                                                h_hi[:, k, half * HALF:(half + 1) * HALF], h_lo[:, k, half * HALF:(half + 1) * HALF],
                                                first=k == 0, last=k == KC - 1)
                        last.then_inc(n_z, 1)

                moments(total, n_mean)
                project(0)
                project(1)
                pe.wait_ge(n_sum, KC)
                moments(total, n_var)
                for c in range(2, KC):
                    project(c)

            @block.scalar
            def _(act):
                def split(c):
                    act.wait_ge(n_raw[c % 2], 16 * (c // 2 + 1))
                    if c >= 2:
                        act.wait_ge(n_z, 2 * (c - 1))
                    act.activation(w[c % 2][0][:], raw[c % 2][:], ACT.Copy).then_inc(n_whi, 1)

                def silu_z(c):
                    for half in range(2):
                        act.wait_ge(n_z, 2 * c + half + 1)
                        if c >= 3:
                            act.wait_ge(n_g, c - 2)
                        act.activation(zs[c % 3][:, half * HALF:(half + 1) * HALF], banks[2 * (c % 3) + half][:], ACT.Silu).then_inc(n_zs, 1)

                split(0)
                split(1)
                for c in range(KC):
                    act.wait_ge(n_d, c + 1)
                    if c >= 2:
                        act.wait_ge(n_sum, c - 1)
                    act.activation(tap[c % 2][:], cv[:, c, :], ACT.Square).then_inc(n_sq, 1)
                for c in range(KC):
                    silu_z(c)
                    if c + 2 < KC:
                        split(c + 2)
                    act.wait_ge(n_t, c + 1)
                    if c >= 2:
                        act.wait_ge(n_g, c - 1)
                    act.activation(tap[c % 2][:], cv[:, c, :], ACT.Silu, bias=keep.chan[:, c, TAPS + 2:TAPS + 3],
                                   scale=keep.chan[:, c, TAPS + 1:TAPS + 2]).then_inc(n_s, 1)
                act.wait_ge(n_z, 2 * KC)
                for c in range(KC):
                    act.wait_ge(n_g, c + 1)
                    act.activation(h_hi[:, c, :], cv[:, c, :], ACT.Copy).then_inc(n_ghi, 1)

            @block.gpsimd
            def _(pool):
                for c in range(KC):
                    pool.wait_ge(n_sq, c + 1)
                    if c == 0:
                        pool.wait_ge(n_mean, 1)
                        pool.tensor_copy(total[:], tap[0][:]).then_inc(n_sum, 1)
                    else:
                        pool.wait_ge(n_sum, c)
                        pool.tensor_tensor(total[:], total[:], tap[c % 2][:], ALU.add).then_inc(n_sum, 1)
                pool.wait_ge(n_eps, 1)
                pool.tensor_tensor(rstd[:], rstd[:], keep.minus_half[:, 0:1].broadcast_to([P, SEQ]), ALU.pow).then_inc(n_rstd, 1)

            @block.vector
            def _(dve):
                def split(c):
                    dve.wait_ge(n_whi, c + 1)
                    dve.tensor_tensor(w[c % 2][1][:], raw[c % 2][:], f(w[c % 2][0][:]), ALU.subtract).then_inc(n_wlo, 1)

                split(0)
                split(1)
                dve.wait_ge(n_mean, 1)
                for c in range(KC):
                    for half in range(2):
                        s = slice(half * HALF, (half + 1) * HALF)
                        last = dve.tensor_tensor(cv[:, c, s], cv[:, c, s], mean_bank[half][:], ALU.subtract)
                    last.then_inc(n_d, 1)
                dve.wait_ge(n_var, 1)
                for half in range(2):
                    last = dve.tensor_scalar(rstd[:, half * HALF:(half + 1) * HALF], mean_bank[half][:], LN_EPS, None, ALU.add)
                last.then_inc(n_eps, 1)
                split(2)
                dve.wait_ge(n_rstd, 1)
                for c in range(KC):
                    if c == 0:
                        dve.wait_ge(n_sq, KC)
                    dve.tensor_tensor(cv[:, c, :], cv[:, c, :], rstd[:], ALU.mult).then_inc(n_t, 1)
                    if 3 <= c + 2 < KC:
                        split(c + 2)
                    dve.wait_ge(n_s, c + 1)
                    dve.wait_ge(n_zs, 2 * c + 2)
                    dve.tensor_tensor(cv[:, c, :], tap[c % 2][:], zs[c % 3][:], ALU.mult).then_inc(n_g, 1)
                for c in range(KC):
                    dve.wait_ge(n_ghi, c + 1)
                    dve.tensor_tensor(h_lo[:, c, :], cv[:, c, :], f(h_hi[:, c, :]), ALU.subtract).then_inc(n_glo, 1)
        m.clear()


class Tensors:
    pass


def build(nc, a):
    with ExitStack() as ctx:
        keep = Tensors()
        m = Memory(nc, ctx, "all")
        keep.h = [m.sb(f"h_{n}", [P, KC, SEQ], F32R) for n in ("hi", "lo")]
        keep.ident = m.sb("ident", [P, P])
        keep.minus_half = m.sb("minus_half", [P, 1])
        keep.chan = m.sb("chan", [P, KC, TAPS + 3])
        with ExitStack() as layer0:
            m0 = Memory(nc, layer0, "l0")
            keep.band = m0.sb("band", [P, 2 * P])
            keep.diag = m0.sb("diag", [P, P])
            keep.rope = m0.sb("rope", [P, 2, NT, HD // 2])
            setup(nc, a, keep)
            attention(nc, a, keep)
        keep.x = m.sb("x", [P, NT, DM])
        tail(nc, a, keep, 0)
        conv_norm(nc, a, keep)
        conv(nc, a, keep)
        tail(nc, a, keep, 1)


_INS = ["x", "p", "positions", "pre_norm_g", "post_norm_g", "attn_w_in", "attn_w_out", "conv_w_in", "conv_dw_w",
        "conv_dw_b", "conv_ln_g", "conv_ln_b", "conv_w_out", "ple_w_proj", "ple_w_gate"]


def kernel(**inputs):
    from concourse import bacc
    from concourse.bass_utils import run_bass_kernel_spmd

    nc = bacc.Bacc("TRN2", target_bir_lowering=False, num_devices=1)
    a = Tensors()
    arrays = {}
    for name in _INS:
        arrays[name] = np.ascontiguousarray(inputs[name])
    dram = lambda name, shape, dt, kind: nc.dram_tensor(name, shape, dt, kind=kind).ap()
    a.x, a.p, a.positions, a.pre_norm_g, a.post_norm_g, a.attn_w_in, a.attn_w_out, a.conv_w_in, a.conv_dw_w, \
        a.conv_dw_b, a.conv_ln_g, a.conv_ln_b, a.conv_w_out, a.ple_w_proj, a.ple_w_gate = (
            dram(n, arrays[n].shape, mybir.dt.from_np(arrays[n].dtype), "ExternalInput") for n in _INS)
    a.u = dram("groups_out", (HPAIRS, NG, SEQ, UROW), F32, "Internal")
    a.oz = dram("gated_out", (DM, SEQ), F32, "Internal")
    a.pp = dram("ple_products", (2, SEQ, DM), F32, "Internal")
    a.out = dram("result", (1, SEQ, DM), F32, "ExternalOutput")
    build(nc, a)
    r = run_bass_kernel_spmd(nc, [arrays], core_ids=[0])
    return r.results[0]["result"]
```

```python
from contextlib import ExitStack

import numpy as np
import concourse.bass as bass
from concourse import mybir

F32 = mybir.dt.float32
F32R = mybir.dt.float32r
I32 = mybir.dt.int32
ACT = mybir.ActivationFunctionType
ALU = mybir.AluOpType
AXX = mybir.AxisListType.X

P = 128
SEQ, DM = 1024, 1024
NT = SEQ // P
KC = DM // P
HALF = 512
PLE = 256
HD = 64
HPAIRS = DM // (2 * HD)
NG = 3
DILATION = (1, 4, 16)
LONE = ((0,), (0, 2, 4, 6), tuple(range(8)))
SCALE = HD ** -0.5
NEG = -1e30
THETA = 10000.0
RMS_EPS, LN_EPS = 1e-6, 1e-5
TAPS = 31
UROW = 2 * HD + 4
TWO_PI = 2 * np.pi
PI_A = 6.28125
PI_B = float(np.float32(np.round((TWO_PI - PI_A) * 2 ** 20) / 2 ** 20))
PI_C = float(np.float32(TWO_PI - PI_A - PI_B))
ROUND = 1.5 * 2 ** 23
PI_IN = 3.1415925


def wait(eng, sem, value):
    if isinstance(value, int) and value <= 0:
        return
    eng.wait_ge(sem, value)


def column(eng, value):
    return value if isinstance(value, int) else eng.snap(value)


def f(ap):
    return ap.bitcast(F32)


class Memory:

    def __init__(self, nc, ctx, prefix):
        self.nc, self.ctx, self.prefix, self.sems = nc, ctx, prefix, []

    def sb(self, name, shape, dt=F32):
        return self.ctx.enter_context(self.nc.sbuf_tensor(f"{self.prefix}_{name}", shape, dt))

    def ps(self, name, cols=HALF):
        return self.ctx.enter_context(self.nc.psum_tensor(f"{self.prefix}_{name}", [P, cols], F32))

    def sem(self, name):
        self.sems.append(self.ctx.enter_context(self.nc.semaphore(f"{self.prefix}_{name}")))
        return self.sems[-1]

    def clear(self):
        with self.nc.Block(no_gpsimd_drain=True) as block:
            @block.sync
            def _(sp):
                for s in self.sems:
                    sp.sem_clear(s)


def three_passes(pe, out, lhs_hi, lhs_lo, rhs_hi, rhs_lo, first=True, last=True):
    pe.matmul(out, lhs_hi, rhs_hi, start=first, stop=False)
    pe.matmul(out, lhs_hi, rhs_lo, start=False, stop=False)
    return pe.matmul(out, lhs_lo, rhs_hi, start=False, stop=last)


class PreNorm:
    def __init__(self, m, x, gain, h, banks, ident, minus_half, work=None):
        self.x, self.gain, self.h, self.banks, self.ident, self.minus_half = x, gain, h, banks, ident, minus_half
        work = work or [m.sb(f"pn_work{i}", [P, DM])[:] for i in range(3)]
        self.squares, self.xn = work[0], work[1:]
        self.ssq = m.sb("pn_ssq", [P, NT])
        self.rstd = m.sb("pn_rstd", [P, NT])
        self.s_ssq = m.sem("pn_ssq_done")
        self.s_var = m.sem("pn_var_done")
        self.s_rstd = m.sem("pn_rstd_done")
        self.s_xn = m.sem("pn_xn_done")
        self.s_tr = m.sem("pn_transposed")
        self.s_hi = m.sem("pn_hi_done")
        self.s_lo = m.sem("pn_lo_done")

    def act_squares(self, act, t):
        wait(act, self.s_ssq, t)
        act.activation(self.squares, self.x[:, t, :], ACT.Square, accum_out=self.ssq[:, t:t + 1]).then_inc(self.s_ssq, 1)

    def pool_rstd(self, pool, t):
        pool.wait_ge(self.s_ssq, t + 1)
        c = slice(t, t + 1)
        pool.tensor_scalar(self.rstd[:, c], self.ssq[:, c], 1.0 / DM, RMS_EPS, ALU.mult, ALU.add).then_inc(self.s_var, 1)
        pool.wait_ge(self.s_var, t + 1)
        pool.tensor_tensor(self.rstd[:, c], self.rstd[:, c], self.minus_half, ALU.pow).then_inc(self.s_rstd, 1)

    def dve_scale(self, dve, t):
        dve.wait_ge(self.s_rstd, t + 1)
        wait(dve, self.s_tr, 2 * (t - 1))
        dve.scalar_tensor_tensor(self.xn[t % 2], self.x[:, t, :], self.rstd[:, t:t + 1], self.gain[:],
                                 ALU.mult, ALU.mult).then_inc(self.s_xn, 1)

    def pe_transposes(self, pe, t):
        pe.wait_ge(self.s_xn, t + 1)
        for half in range(2):
            n = 2 * t + half
            wait(pe, self.s_lo, n - 1)
            for k in range(4):
                c = 4 * half + k
                last = pe.transpose(self.banks[half][:, k * P:(k + 1) * P], self.xn[t % 2][:, c * P:(c + 1) * P], self.ident[:])
            last.then_inc(self.s_tr, 1)

    def act_hi(self, act, t):
        for half in range(2):
            act.wait_ge(self.s_tr, 2 * t + half + 1)
            act.activation(self.h[0][:, 4 * half:4 * half + 4, t * P:(t + 1) * P],
                           self.banks[half][:].rearrange("p (k n) -> p k n", k=4), ACT.Copy).then_inc(self.s_hi, 1)

    def dve_lo(self, dve, t):
        for half in range(2):
            dve.wait_ge(self.s_hi, 2 * t + half + 1)
            sl = (slice(None), slice(4 * half, 4 * half + 4), slice(t * P, (t + 1) * P))
            dve.tensor_tensor(self.h[1][sl], self.banks[half][:].rearrange("p (k n) -> p k n", k=4),
                              f(self.h[0][sl]), ALU.subtract).then_inc(self.s_lo, 1)


class FirstWeights:

    def __init__(self, m, w_out, w, raw):
        self.src, self.w, self.raw = w_out.rearrange("(k p) c -> p k c", p=P), w, raw
        self.s_in = m.sem("fw_in")
        self.s_hi = m.sem("fw_hi_done")
        self.s_lo = m.sem("fw_lo_done")

    def load(self, eng):
        for n in range(4):
            eng.dma_start(self.raw[n], self.src[:, 2 * n:2 * n + 2, 0:HALF]).then_inc(self.s_in, 16)

    def act_hi(self, act, n):
        act.wait_ge(self.s_in, 64)
        act.activation(self.w[0][:, 2 * n:2 * n + 2, :], self.raw[n], ACT.Copy).then_inc(self.s_hi, 1)

    def dve_lo(self, dve, n):
        dve.wait_ge(self.s_hi, n + 1)
        dve.tensor_tensor(self.w[1][:, 2 * n:2 * n + 2, :], self.raw[n], f(self.w[0][:, 2 * n:2 * n + 2, :]), ALU.subtract).then_inc(self.s_lo, 1)


def setup(nc, a, keep):
    with ExitStack() as ctx:
        m = Memory(nc, ctx, "su")
        x = m.sb("x", [P, NT, DM])
        gain = m.sb("gain", [P, DM])
        pos_i = m.sb("pos_i", [P, NT], I32)
        pos = m.sb("pos", [P, NT])
        inv_freq = m.sb("inv_freq", [P, HD // 2])
        p_in = [m.sb(f"p_in{l}", [P, NT, PLE]) for l in range(2)]
        pT = [m.sb(f"pT_{w}", [P, PLE // P, SEQ], F32R) for w in ("hi", "lo")]
        w_raw = [m.sb(f"w_raw{l}", [P, PLE // P, DM]) for l in range(2)]
        ws = [[m.sb(f"w{l}_{n}", [P, PLE // P, DM], F32R) for n in ("hi", "lo")] for l in range(2)]
        split_t = lambda ap: ap.rearrange("p (t c) -> p t c", t=NT)
        angle = split_t(p_in[0][:, 0, :])
        turns = [split_t(p_in[0][:, 1 + q, :]) for q in range(2)]
        rows = w_raw[0][0:TAPS + 3, 0, :]
        out = [m.sb(f"out{i}", [P, HALF]) for i in range(4)]
        bank_t = [m.ps(f"bank_t{i}") for i in range(2)]
        bank_p = [m.ps(f"bank_p{i}") for i in range(2)]
        bank_o = [m.ps(f"bank_o{i}") for i in range(4)]
        s_const = m.sem("constants_set")
        s_cchain = m.sem("constants_chain")
        s_pos = m.sem("positions_in")
        s_gain = m.sem("gain_in")
        s_x = [m.sem(f"x_in{t}") for t in range(NT)]
        s_p = [m.sem(f"p_in{l}") for l in range(2)]
        s_w = [m.sem(f"w_in{l}") for l in range(2)]
        s_rows = m.sem("rows_in")
        s_ct = m.sem("rows_transposed")
        s_chan = m.sem("channels_done")
        s_rope = m.sem("rope_chain")
        s_sin = m.sem("sines_done")
        s_pt = m.sem("p_transposed")
        s_phi = m.sem("p_hi_done")
        s_plo = m.sem("p_lo_done")
        s_whi = m.sem("w_hi_done")
        s_wlo = m.sem("w_lo_done")
        s_mm = m.sem("products_done")
        s_out = m.sem("products_copied")
        s_st = [m.sem(f"product_stored{i}") for i in range(4)]
        pn = PreNorm(m, x, gain, keep.h, bank_t, keep.ident, keep.minus_half[:, 0:1])
        DEPTH = 2

        with nc.Block() as block:
            @block.sync
            def _(sp):
                def layer_in(l):
                    sp.dma_start(w_raw[l][:], a.ple_w_proj[l].rearrange("(k p) c -> p k c", p=P)).then_inc(s_w[l], 16)
                    sp.dma_start(p_in[l][:], a.p[l, 0].rearrange("(t p) c -> p t c", p=P)).then_inc(s_p[l], 16)

                sp.dma_start(x[:, 0, :], a.x[0, 0:P, :]).then_inc(s_x[0], 16)
                sp.dma_start(gain[:], a.pre_norm_g[0, :].partition_broadcast(P)).then_inc(s_gain, 16)
                layer_in(0)
                for t in range(1, NT):
                    sp.dma_start(x[:, t, :], a.x[0, t * P:(t + 1) * P, :]).then_inc(s_x[t], 16)
                layer_in(1)
                sp.dma_start(pos_i[:], a.positions.rearrange("b (t p) -> p (b t)", p=P), allow_slow_non_contiguous=True).then_inc(s_pos, 16)
                sp.wait_ge(s_wlo, 2)
                sp.dma_start(rows[0:TAPS, :], a.conv_dw_w[0]).then_inc(s_rows, 16)
                for i, r in enumerate((a.conv_dw_b, a.conv_ln_g, a.conv_ln_b)):
                    sp.dma_start(rows[TAPS + i:TAPS + i + 1, :], r[0:1, :]).then_inc(s_rows, 16)
                for i in range(2 * NT * DEPTH):
                    l, t, half = i // (2 * NT), i // 2 % NT, i % 2
                    sp.wait_ge(s_out, i + 1)
                    sp.dma_start(a.pp[l, t * P:(t + 1) * P, half * HALF:(half + 1) * HALF], out[i % 4][:]).then_inc(s_st[i % 4], 16)
                for i in range(4):
                    sp.wait_ge(s_st[i], 16 * DEPTH * NT // 2)

            @block.gpsimd
            def _(pool):
                pool.memset(keep.minus_half[:], -0.5).then_inc(s_const, 1)
                pool.memset(keep.ident[:], 0.0).then_inc(s_cchain, 1)
                pool.memset(keep.band[:], 0.0).then_inc(s_cchain, 1)
                pool.memset(keep.diag[:], 0.0).then_inc(s_cchain, 1)
                pool.wait_ge(s_cchain, 3)
                pool.affine_select(out=keep.ident[:], in_=keep.ident[:], compare_op=ALU.not_equal, fill=1.0,
                                   base=0, pattern=[[-1, P]], channel_multiplier=1).then_inc(s_const, 1)
                pool.affine_select(out=keep.band[:], in_=keep.band[:], compare_op=ALU.is_ge, fill=NEG,
                                   base=P, pattern=[[-1, 2 * P]], channel_multiplier=1).then_inc(s_cchain, 1)
                pool.affine_select(out=keep.diag[:], in_=keep.diag[:], compare_op=ALU.is_ge, fill=NEG,
                                   base=0, pattern=[[-1, P]], channel_multiplier=1).then_inc(s_cchain, 1)
                pool.wait_ge(s_cchain, 5)
                pool.affine_select(out=keep.band[:], in_=keep.band[:], compare_op=ALU.is_ge, fill=NEG,
                                   base=0, pattern=[[1, 2 * P]], channel_multiplier=-1)
                pool.affine_select(out=keep.diag[:, 0:HD], in_=keep.diag[:, 0:HD], compare_op=ALU.is_ge, fill=NEG,
                                   base=HD - 1, pattern=[[0, HD]], channel_multiplier=-1)
                for i in range(HD // 2):
                    v = float(np.float32(1.0) / np.float32(THETA ** (2 * i / HD)))
                    last = pool.memset(inv_freq[:, i:i + 1], v)
                last.then_inc(s_const, 1)
                for t in range(NT):
                    pn.pool_rstd(pool, t)

            @block.vector
            def _(dve):
                links = [0]

                def link(op):
                    links[0] += 1
                    op.then_inc(s_rope, 1)
                    dve.wait_ge(s_rope, links[0])

                def w_lo(l):
                    dve.wait_ge(s_whi, 2 * l + 2)
                    for k in range(2):
                        dve.tensor_tensor(ws[l][1][:, k, :], w_raw[l][:, k, :], f(ws[l][0][:, k, :]), ALU.subtract).then_inc(s_wlo, 1)

                def p_lo(n):
                    l, t = n // NT, n % NT
                    dve.wait_ge(s_phi, n + 1)
                    dve.tensor_tensor(pT[1][:, :, t * P:(t + 1) * P], bank_p[t % 2][:, 0:2 * P].rearrange("p (k n) -> p k n", k=2),
                                      f(pT[0][:, :, t * P:(t + 1) * P]), ALU.subtract).then_inc(s_plo, 1)

                dve.wait_ge(s_gain, 16)
                for n in range(DEPTH * NT):
                    if n % NT == 0:
                        w_lo(n // NT)
                    p_lo(n)
                    if n < NT:
                        pn.dve_scale(dve, n)
                    if 1 <= n <= NT:
                        pn.dve_lo(dve, n - 1)
                dve.wait_ge(s_pos, 16)
                dve.wait_ge(s_const, 3)
                link(dve.tensor_copy(pos[:], pos_i[:]))
                for t in range(NT):
                    last = dve.tensor_scalar(angle[:, t, :], inv_freq[:], pos[:, t:t + 1], None, ALU.mult)
                link(last)
                for q in range(2):
                    link(dve.tensor_scalar(turns[q], angle, 1.0 / TWO_PI, 0.25 * q, ALU.mult, ALU.add))
                    link(dve.tensor_scalar(turns[q], turns[q], ROUND, None, ALU.add))
                    link(dve.tensor_scalar(turns[q], turns[q], ROUND, None, ALU.subtract))
                    rest = keep.rope[:, q]
                    link(dve.scalar_tensor_tensor(rest, turns[q], -PI_A, angle, ALU.mult, ALU.add))
                    link(dve.scalar_tensor_tensor(rest, turns[q], -PI_B, rest, ALU.mult, ALU.add))
                    link(dve.scalar_tensor_tensor(rest, turns[q], -PI_C, rest, ALU.mult, ALU.add))
                    link(dve.tensor_scalar(rest, rest, float(q * np.pi / 2), PI_IN, ALU.add, ALU.min))
                    link(dve.tensor_scalar(rest, rest, -PI_IN, None, ALU.max))
                dve.wait_ge(s_ct, 1)
                dve.tensor_copy(keep.chan[:].rearrange("p c n -> p (c n)"), bank_o[0][:, 0:KC * (TAPS + 3)]).then_inc(s_chan, 1)

            @block.scalar
            def _(act):
                def squares(t):
                    act.wait_ge(s_x[t], 16)
                    pn.act_squares(act, t)

                def w_hi(l):
                    act.wait_ge(s_w[l], 16)
                    for k in range(2):
                        act.activation(ws[l][0][:, k, :], w_raw[l][:, k, :], ACT.Copy).then_inc(s_whi, 1)

                def p_hi(n):
                    l, t = n // NT, n % NT
                    act.wait_ge(s_pt, n + 1)
                    wait(act, s_mm, 2 * (n - NT + 1))
                    act.activation(pT[0][:, :, t * P:(t + 1) * P], bank_p[t % 2][:, 0:2 * P].rearrange("p (k n) -> p k n", k=2),
                                   ACT.Copy).then_inc(s_phi, 1)

                squares(0)
                w_hi(0)
                p_hi(0)
                for n in range(DEPTH * NT):
                    if n + 1 == NT:
                        w_hi(1)
                    if n + 1 < DEPTH * NT:
                        p_hi(n + 1)
                    if n + 1 < NT:
                        squares(n + 1)
                    if 1 <= n <= NT:
                        pn.act_hi(act, n - 1)
                    for half in range(2):
                        i = 2 * n + half
                        act.wait_ge(s_mm, i + 1)
                        wait(act, s_st[i % 4], 16 * (i // 4))
                        act.activation(out[i % 4][:], bank_o[i % 4][:], ACT.Copy).then_inc(s_out, 1)
                act.wait_ge(s_rope, 18)
                act.activation(keep.rope[:], keep.rope[:], ACT.Sin).then_inc(s_sin, 1)

            @block.tensor
            def _(pe):
                pe.wait_ge(s_const, 2)

                def p_transposes(n):
                    l, t = n // NT, n % NT
                    pe.wait_ge(s_p[l], 16)
                    wait(pe, s_plo, n - 1)
                    for k in range(2):
                        last = pe.transpose(bank_p[t % 2][:, k * P:(k + 1) * P], p_in[l][:, t, k * P:(k + 1) * P], keep.ident[:])
                    last.then_inc(s_pt, 1)

                p_transposes(0)
                p_transposes(1)
                for n in range(DEPTH * NT):
                    l, t = n // NT, n % NT
                    if n + 2 < DEPTH * NT:
                        p_transposes(n + 2)
                    if 1 <= n <= NT:
                        pn.pe_transposes(pe, n - 1)
                    pe.wait_ge(s_plo, n + 1)
                    pe.wait_ge(s_wlo, 2 * l + 2)
                    for half in range(2):
                        i = 2 * n + half
                        wait(pe, s_out, i - 3)
                        for k in range(2):
                            last = three_passes(pe, bank_o[i % 4][:], pT[0][:, k, t * P:(t + 1) * P], pT[1][:, k, t * P:(t + 1) * P],
                                                ws[l][0][:, k, half * HALF:(half + 1) * HALF], ws[l][1][:, k, half * HALF:(half + 1) * HALF],
                                                first=k == 0, last=k == 1)
                        last.then_inc(s_mm, 1)
                nrow = TAPS + 3
                pe.wait_ge(s_rows, 64)
                pe.wait_ge(s_out, 2 * NT * DEPTH - 3)
                for c in range(KC):
                    last = pe.transpose(bank_o[0][:, c * nrow:(c + 1) * nrow], rows[:, c * P:(c + 1) * P], keep.ident[0:nrow, 0:nrow])
                last.then_inc(s_ct, 1)
        m.clear()


def attention(nc, a, keep):
    h_hi, h_lo = keep.h
    with ExitStack() as ctx:
        m = Memory(nc, ctx, "at")
        raw = [m.sb(f"raw{i}", [P, KC, P]) for i in range(2)]
        wqk = [w[:, :, 0:2 * P] for w in keep.w]
        wv = [[w[:, :, (2 + i) * P:(3 + i) * P] for w in keep.w] for i in range(2)]
        qk = [[m.sb(f"qk{g}_{n}", [P, 2, SEQ], F32R) for n in ("hi", "lo")] for g in range(NG)]
        vT = m.sb("vT", [P, SEQ])
        v = m.sb("v", [P, NT, 2, 2, HD], F32R)
        turned_all = m.sb("turned", [P, 2, 2, 2 * P])
        turned = [turned_all[:, i] for i in range(2)]
        rotated = [m.sb(f"rotated{i}", [P, 2 * P]) for i in range(2)]
        prob = [m.sb(f"prob{i}", [P, 2, 2 * P]) for i in range(2)]
        probT = [[m.sb(f"probT{i}_{n}", [P, 4, P], F32R) for n in ("hi", "lo")] for i in range(2)]
        bias = [m.sb(f"bias{i}", [P, 2]) for i in range(2)]
        urow = [m.sb(f"urow{i}", [P, UROW]) for i in range(4)]
        mix_all = m.sb("mix", [P, 2, 4 * NG, UROW])
        mix = [mix_all[:, q] for q in range(2)]
        mmax = m.sb("mmax", [P, 4, 2])
        mw = m.sb("mw", [P, 4, NG, 2])
        msw = m.sb("msw", [P, 4, NG, 2])
        mden = m.sb("mden", [P, 4, 2])
        siluz = m.sb("siluz", [P, SEQ])
        bank_p = [m.ps(f"bank_p{i}") for i in range(2)]
        bank_s = m.ps("bank_s", 2 * HALF)
        bank_pt = m.ps("bank_pt")
        bank_o = m.ps("bank_o")
        bank_qk = m.ps("bank_qk")
        bank_vo = m.ps("bank_vo")

        s_raw = [m.sem(f"raw_in{i}") for i in range(2)]
        s_whi = m.sem("w_hi_done")
        s_wlo = m.sem("w_lo_done")
        s_qkp = m.sem("qk_projected")
        s_vp = m.sem("v_projected")
        s_zp = m.sem("z_projected")
        s_turn = m.sem("qk_turned")
        s_rot1 = m.sem("qk_rotated_half")
        s_rot = m.sem("qk_rotated")
        s_qkt = m.sem("qk_transposed")
        s_qkhi = m.sem("qk_hi_done")
        s_qklo = m.sem("qk_lo_done")
        s_vT = m.sem("v_copied")
        s_vt = m.sem("v_transposed")
        s_vhi = m.sem("v_hi_done")
        s_vlo = m.sem("v_lo_done")
        s_ez = m.sem("z_exp_done")
        s_zchain = m.sem("z_chain")
        s_z = m.sem("z_silu_done")
        s_sc = m.sem("scores_done")
        s_mask = m.sem("scores_masked")
        s_max = m.sem("max_done")
        s_bias = m.sem("bias_done")
        s_exp = m.sem("exp_done")
        s_ptr = m.sem("prob_transposed")
        s_pthi = m.sem("probT_hi_done")
        s_ptlo = m.sem("probT_lo_done")
        s_pv = m.sem("pv_done")
        s_uhi = m.sem("urow_copied")
        s_u = m.sem("urow_done")
        s_ust = [m.sem(f"urow_stored{i}") for i in range(4)]
        s_stored = m.sem("pair_stored")
        s_mix = [m.sem(f"mix_in{q}") for q in range(2)]
        s_mc = m.sem("mix_chain")
        s_md = m.sem("mix_difference_done")
        s_mw = m.sem("mix_weights_exp")
        s_mcoef = m.sem("mix_coefficients_done")
        s_mm = m.sem("mix_products_done")
        s_ma = m.sem("mix_first_sum_done")
        s_mo = m.sem("mixed")
        s_ot = m.sem("mixed_transposed")
        s_oz = m.sem("gated")
        s_ozst = m.sem("gated_stored")
        s_oin = [m.sem(f"gated_in{i}") for i in range(2)]
        s_ohi = m.sem("gated_hi_done")
        s_olo = m.sem("gated_lo_done")
        free = [mix_all[:].rearrange("p q n c -> p (q n c)")[:, i * DM:(i + 1) * DM] for i in range(3)]
        free.append(turned_all[:].rearrange("p i q n -> p (i q n)"))
        fw = FirstWeights(m, a.attn_w_out[0], keep.w, [b.rearrange("p (k n) -> p k n", k=2) for b in free])

        NCH = 10
        COL = [0, 3 * DM, 6 * DM, DM, 4 * DM, 7 * DM, 2 * DM, 5 * DM, 8 * DM, 9 * DM]
        PLACE = [(wqk, 0), (wqk, P), (wv[0], 0), (wqk, 0), (wqk, P), (wv[1], 0), (wqk, 0), (wqk, P), (wv[0], 0), (wv[1], 0)]
        w_in = a.attn_w_in[0].rearrange("(k p) c -> p k c", p=P)


        def prev_blocks(g, b):
            return (1,) if b in LONE[g] else (0, 1)

        def perm2(buf, g, start, n):
            d = DILATION[g]
            return buf.rearrange("p (r m) -> p m r", r=d)[:, start // d:(start + n) // d, :]

        def perm3(buf, g, start, n):
            d = DILATION[g]
            return buf.rearrange("p x (r m) -> p x m r", r=d)[:, :, start // d:(start + n) // d, :]

        def rows(hp, g, b):
            d = DILATION[g]
            base = a.u[bass.ds(hp, 1), g]
            r = base.rearrange("h (m r) c -> (h r) m c", r=d)
            L = SEQ // d
            if L >= P:
                return r[(P * b) // L, (P * b) % L:(P * b) % L + P, :]
            return r[P // L * b:P // L * (b + 1)]

        def bodies(eng, body):
            body(0, first=True)
            body(1)
            with eng.Fori(2, HPAIRS - 1) as hp:
                body(hp)
            body(HPAIRS - 1, last=True)
            body(HPAIRS, after=True)

        with nc.Block() as block:
            @block.sync
            def _(sp):
                def load(hp, j):
                    if j >= NCH:
                        hp, j = hp + 1, j - NCH
                    at = column(sp, hp * P + COL[j])
                    wait(sp, s_wlo, NCH * hp + j - 1)
                    sp.dma_start(raw[j % 2][:], w_in[:, :, bass.ds(at, P)]).then_inc(s_raw[j % 2], 16)

                def store(hp, g, b):
                    hp, g = (hp - 1, 2) if g == 0 else (hp, g - 1)
                    pair = column(sp, hp)
                    sp.wait_ge(s_u, NT * (NG * hp + g) + b + 1)
                    sp.dma_start(rows(pair, g, b), urow[b % 4][:]).then_inc(s_ust[b % 4], 16)

                def body(hp, first=False, last=False, after=False):
                    proj = not after
                    for g in range(NG if proj else 2):
                        att = not (first and g == 0) and not (after and g > 0)
                        if proj:
                            load(hp, 3 * g + 3)
                        for s in range(NT):
                            if proj and s == 4 and not (last and g == 2):
                                load(hp, 3 * g + 4)
                            if g == 2 and s == 5 and not last:
                                load(hp, 11)
                            if att and s >= 2:
                                store(hp, g, s - 2)
                            if after and g == 0 and s < HPAIRS - 1:
                                if s >= 2:
                                    sp.wait_ge(s_olo, s - 1)
                                else:
                                    sp.wait_ge(s_wlo, NCH * HPAIRS)
                                sp.wait_ge(s_ozst, 16 * (HPAIRS - 1))
                                sp.dma_start(raw[s % 2][:].rearrange("p k n -> p (k n)"), a.oz[s * P:(s + 1) * P, :]).then_inc(s_oin[s % 2], 16)
                        if g < 2 and proj:
                            load(hp, 3 * g + 5)
                        elif proj and not last:
                            load(hp, 12)
                        if att:
                            for b in range(NT - 2, NT):
                                store(hp, g, b)
                        if g == 0 and not first:
                            pair = column(sp, hp - 1)
                            for i in range(4):
                                sp.wait_ge(s_ust[i], 16 * 2 * NG * hp)
                            if after:
                                sp.wait_ge(fw.s_lo, 4)
                            sp.sem_inc(s_stored, 1)
                            for q in range(2):
                                for t in range(4):
                                    sp.dma_start(mix[q][:, t * NG:(t + 1) * NG, :],
                                                 a.u[bass.ds(pair, 1), :, (4 * q + t) * P:(4 * q + t + 1) * P, :]
                                                 .rearrange("h g p c -> p (h g) c")).then_inc(s_mix[q], 16)
                        if g == 1 and not first and not after:
                            row = column(sp, (hp - 1) * P)
                            sp.wait_ge(s_oz, 2 * hp)
                            sp.dma_start(a.oz[bass.ds(row, P), :], siluz[:]).then_inc(s_ozst, 16)

                load(0, 0)
                load(0, 1)
                load(0, 2)
                bodies(sp, body)

            @block.gpsimd
            def _(pool):
                def rotate(hp, g, s):
                    n = NT * (NG * hp + g) + s
                    pool.wait_ge(s_turn, n + 1)
                    wait(pool, s_qkt, n - 1)
                    src = turned[s % 2].rearrange("p w (h x i) -> p w h x i", x=2, i=HD // 2)
                    dst = rotated[s % 2][:].rearrange("p (h x i) -> p h x i", x=2, i=HD // 2)
                    pool.tensor_tensor(dst[:, :, 0, :], src[:, 1, :, 0, :], src[:, 0, :, 1, :], ALU.subtract).then_inc(s_rot1, 1)
                    pool.tensor_tensor(dst[:, :, 1, :], src[:, 1, :, 1, :], src[:, 0, :, 0, :], ALU.add).then_inc(s_rot, 1)

                def mixture(hp, q):
                    k = 2 * hp + q
                    pool.wait_ge(s_mcoef, k + 1)
                    u = mix[q][:, :, 0:2 * HD].rearrange("p n (e d) -> p n e d", e=2)
                    c = msw[:].rearrange("p t g e -> p (t g) e").unsqueeze(3).broadcast_to([P, 4 * NG, 2, HD])
                    pool.tensor_tensor(u, u, c, ALU.mult).then_inc(s_mm, 1)
                    pool.wait_ge(s_mm, k + 1)
                    ug = mix[q].rearrange("p (t g) c -> p t g c", g=NG)
                    pool.tensor_tensor(ug[:, :, 0, 0:P], ug[:, :, 0, 0:P], ug[:, :, 1, 0:P], ALU.add).then_inc(s_ma, 1)
                    pool.wait_ge(s_ma, k + 1)
                    pool.tensor_tensor(ug[:, :, 0, 0:P], ug[:, :, 0, 0:P], ug[:, :, 2, 0:P], ALU.add).then_inc(s_mo, 1)

                def body(hp, first=False, last=False, after=False):
                    if after:
                        pool.wait_ge(s_rot, NT * NG * HPAIRS)
                        pool.wait_ge(s_ot, 2 * (HPAIRS - 1))
                        fw.load(pool)
                    for g in range(NG if not after else 2):
                        for s in range(NT):
                            if not after:
                                rotate(hp, g, s)
                            if g == 1 and not first and s in (3, 6):
                                mixture(hp - 1, s // 6)

                bodies(pool, body)

            @block.tensor
            def _(pe):
                def project_qk(hp, g, s, part, first):
                    n = NT * (NG * hp + g) + s
                    if part:
                        pass
                    elif s >= 2:
                        pe.wait_ge(s_turn, n - 1)
                    elif not (first and g == 0):
                        pe.wait_ge(s_vT, 2 * (NG * hp + g - 1) + s + 1)
                    if s == 0 and part == 0:
                        pe.wait_ge(s_wlo, NCH * hp + 3 * g + 2)
                    for k in range(part * KC // 2, (part + 1) * KC // 2):
                        last = three_passes(pe, bank_p[s % 2][:, 0:2 * P], h_hi[:, k, s * P:(s + 1) * P], h_lo[:, k, s * P:(s + 1) * P],
                                            wqk[0][:, k, :], wqk[1][:, k, :], first=k == 0, last=k == KC - 1)
                    if part:
                        last.then_inc(s_qkp, 1)

                def transpose_qk(hp, g, s):
                    n = NT * (NG * hp + g) + s
                    pe.wait_ge(s_rot, n + 1)
                    wait(pe, s_qklo, n)
                    for x in range(2):
                        last = pe.transpose(bank_qk[:, x * P:(x + 1) * P], rotated[s % 2][:, x * P:(x + 1) * P], keep.ident[:])
                    last.then_inc(s_qkt, 1)

                def project_v(hp, g, half, z=False):
                    V = 4 * hp + (3 if z else g)
                    if g == 2 and not z:
                        pe.wait_ge(s_z, 2 * hp + half + 1)
                    else:
                        pe.wait_ge(s_turn, NT * (NG * hp + g) + 7 + half)
                    pe.wait_ge(s_wlo, NCH * hp + (10 if z else 3 * g + 3))
                    slot = wv[(3 if z else g) % 2]
                    for k in range(KC):
                        last = three_passes(pe, bank_p[half][:], slot[0][:, k, :], slot[1][:, k, :],
                                            h_hi[:, k, half * HALF:(half + 1) * HALF], h_lo[:, k, half * HALF:(half + 1) * HALF],
                                            first=k == 0, last=k == KC - 1)
                    last.then_inc(s_zp if z else s_vp, 1)

                def unit_before(hp, g):
                    return (hp - 1, 2) if g == 0 else (hp, g - 1)

                def transpose_v(hp, g, q):
                    A = NG * hp + g
                    if q == 0:
                        pe.wait_ge(s_vT, 2 * A + 2)
                        if g == 1:
                            wait(pe, s_oz, 2 * hp)
                    wait(pe, s_vlo, 2 * A + q)
                    for b in range(4):
                        c = (4 * q + b) * P
                        last = pe.transpose(bank_vo[:, b * P:(b + 1) * P], vT[:, c:c + P], keep.ident[:])
                    last.then_inc(s_vt, 1)

                def scores(hp, g, b):
                    A = NG * hp + g
                    n = NT * A + b
                    if b == 0:
                        pe.wait_ge(s_qklo, NT * A + NT)
                    wait(pe, s_mask, n)
                    j0 = prev_blocks(g, b)[0]
                    for e in range(2):
                        row = slice(e * HD, (e + 1) * HD)
                        q_ = [w[row, 0, b * P:(b + 1) * P] for w in qk[g]]
                        k_ = [w[row, 1, (b - 1 + j0) * P:(b + 1) * P] for w in qk[g]]
                        last = three_passes(pe, bank_s[:, e * HALF + j0 * P:e * HALF + 2 * P], q_[0], q_[1], k_[0], k_[1])
                    last.then_inc(s_sc, 1)

                def transpose_prob(hp, g, b):
                    n = NT * (NG * hp + g) + b
                    pe.wait_ge(s_exp, n + 1)
                    wait(pe, s_ptlo, n)
                    for e in range(2):
                        for j in prev_blocks(g, b):
                            last = pe.transpose(bank_pt[:, (2 * e + j) * P:(2 * e + j + 1) * P], prob[b % 2][:, e, j * P:(j + 1) * P], keep.ident[:])
                    last.then_inc(s_ptr, 1)

                def times_v(hp, g, b):
                    A = NG * hp + g
                    n = NT * A + b
                    if b % 4 == 0:
                        pe.wait_ge(s_vlo, 2 * A + b // 4 + 1)
                    pe.wait_ge(s_ptlo, n + 1)
                    wait(pe, s_u, n)
                    js = prev_blocks(g, b)
                    for e in range(2):
                        for j in js:
                            ve = v[:, b - 1 + j, e]
                            pe.matmul(bank_o[:, e * P:(e + 1) * P], probT[b % 2][0][:, 2 * e + j, :], ve.rearrange("p w n -> p (w n)"),
                                      start=j == js[0], stop=False)
                            last = pe.matmul(bank_o[:, e * P:e * P + HD], probT[b % 2][1][:, 2 * e + j, :], ve[:, 0, :],
                                             start=False, stop=j == 1)
                    last.then_inc(s_pv, 1)

                def transpose_mixed(hp, q):
                    pe.wait_ge(s_mo, 2 * hp + q + 1)
                    if q == 0:
                        all_v = isinstance(hp, int) and hp == HPAIRS - 1
                        pe.wait_ge(s_vlo, 2 * NG * HPAIRS if all_v else 2 * NG * (hp + 1) + 2)
                    else:
                        pe.wait_ge(s_oz, 2 * hp + 1)
                    for t in range(4):
                        last = pe.transpose(bank_vo[:, t * P:(t + 1) * P], mix[q][:, t * NG, 0:P], keep.ident[:])
                    last.then_inc(s_ot, 1)

                def body(hp, first=False, last=False, after=False):
                    proj = not after
                    for g in range(NG if proj else 2):
                        att = not (first and g == 0) and not (after and g > 0)
                        ah, ag = unit_before(hp, g)
                        for s in range(NT):
                            if att:
                                scores(ah, ag, s)
                            if proj:
                                project_qk(hp, g, s, 0, first)
                            if att and s < 2:
                                transpose_v(ah, ag, s)
                            if att and s >= 1:
                                times_v(ah, ag, s - 1)
                            if proj:
                                project_qk(hp, g, s, 1, first)
                            if att:
                                transpose_prob(ah, ag, s)
                            if proj and s >= 1:
                                transpose_qk(hp, g, s - 1)
                        if proj:
                            project_v(hp, g, 0, z=g == 2)
                        if att:
                            times_v(ah, ag, NT - 1)
                        if proj:
                            transpose_qk(hp, g, NT - 1)
                        if g == 1 and not first:
                            transpose_mixed(hp - 1, 0)
                        if proj:
                            project_v(hp, g, 1, z=g == 2)
                        if g == 1 and not first:
                            transpose_mixed(hp - 1, 1)
                        if g == 2:
                            project_v(hp, g, 0)
                            project_v(hp, g, 1)

                pe.wait_ge(s_wlo, 2)
                bodies(pe, body)

            @block.scalar
            def _(act):
                def split(hp, j):
                    if j >= NCH:
                        hp, j = hp + 1, j - NCH
                    act.wait_ge(s_raw[j % 2], 16 * (5 * hp + j // 2 + 1))
                    if j in (2, 5, 8, 9):
                        if j == 9:
                            act.wait_ge(s_vp, 6 * hp + 4)
                        elif j == 5:
                            wait(act, s_zp, 2 * hp)
                        else:
                            wait(act, s_vp, 6 * hp + (0 if j == 2 else 2))
                    else:
                        wait(act, s_qkp, NT * (NG * hp + j // 3))
                    dst, c = PLACE[j]
                    act.activation(dst[0][:, :, c:c + P], raw[j % 2][:], ACT.Copy).then_inc(s_whi, 1)

                def qk_hi(hp, g, s):
                    n = NT * (NG * hp + g) + s
                    act.wait_ge(s_qkt, n + 1)
                    act.activation(perm3(qk[g][0][:], g, s * P, P),
                                   bank_qk[:, 0:2 * P].rearrange("p (x m r) -> p x m r", x=2, r=DILATION[g]), ACT.Copy).then_inc(s_qkhi, 1)

                def v_copy(hp, g, half):
                    U = NG * hp + g
                    act.wait_ge(s_vp, 2 * U + half + 1)
                    wait(act, s_vt, 2 * U)
                    act.activation(perm2(vT[:], g, half * HALF, HALF),
                                   bank_p[half][:].rearrange("p (m r) -> p m r", r=DILATION[g]), ACT.Copy).then_inc(s_vT, 1)

                def v_hi(hp, g, q):
                    act.wait_ge(s_vt, 2 * (NG * hp + g) + q + 1)
                    act.activation(v[:, 4 * q:4 * q + 4, :, 0, :], bank_vo[:].rearrange("p (b e n) -> p b e n", b=4, e=2), ACT.Copy).then_inc(s_vhi, 1)

                def z_exp(hp, half):
                    act.wait_ge(s_zp, 2 * hp + half + 1)
                    wait(act, s_ozst, 16 * hp)
                    act.activation(siluz[:, half * HALF:(half + 1) * HALF], bank_p[half][:], ACT.Exp, scale=-1.0).then_inc(s_ez, 1)

                def exps(hp, g, b):
                    n = NT * (NG * hp + g) + b
                    act.wait_ge(s_bias, n + 1)
                    j0 = prev_blocks(g, b)[0]
                    for e in range(2):
                        row = prob[b % 2][:, e, j0 * P:2 * P]
                        last = act.activation(row, row, ACT.Exp, bias=bias[b % 2][:, e:e + 1], scale=SCALE,
                                              accum_out=urow[b % 4][:, 2 * HD + 2 + e:2 * HD + 3 + e])
                    last.then_inc(s_exp, 1)

                def probT_hi(hp, g, b):
                    n = NT * (NG * hp + g) + b
                    act.wait_ge(s_ptr, n + 1)
                    wait(act, s_pv, n - 1)
                    j0 = prev_blocks(g, b)[0]
                    act.activation(probT[b % 2][0][:].rearrange("p (e j) n -> p e j n", e=2)[:, :, j0:2, :],
                                   bank_pt[:].rearrange("p (e j n) -> p e j n", e=2, j=2)[:, :, j0:2, :], ACT.Copy).then_inc(s_pthi, 1)

                def u_copy(hp, g, b):
                    n = NT * (NG * hp + g) + b
                    act.wait_ge(s_pv, n + 1)
                    act.activation(urow[b % 4][:, 0:2 * HD].rearrange("p (e n) -> p e n", e=2),
                                   bank_o[:, 0:2 * P].rearrange("p (e w n) -> p e w n", e=2, w=2)[:, :, 0, :], ACT.Copy).then_inc(s_uhi, 1)

                def gated_hi(c):
                    act.wait_ge(s_vp, 2 * NG * HPAIRS)
                    act.wait_ge(s_oin[c % 2], 16 * (c // 2 + 1))
                    act.activation(h_hi[:, c, :], raw[c % 2][:].rearrange("p k n -> p (k n)"), ACT.Copy).then_inc(s_ohi, 1)

                def mix_exp(hp, q):
                    act.wait_ge(s_md, 2 * hp + q + 1)
                    act.activation(mw[:], mw[:], ACT.Exp, scale=SCALE).then_inc(s_mw, 1)

                def unit_before(hp, g):
                    return (hp - 1, 2) if g == 0 else (hp, g - 1)

                def body(hp, first=False, last=False, after=False):
                    proj = not after
                    for g in range(NG if proj else 2):
                        att = not (first and g == 0) and not (after and g > 0)
                        ah, ag = unit_before(hp, g)
                        for s in range(NT):
                            if att and s >= 1:
                                probT_hi(ah, ag, s - 1)
                            if proj and s >= 2:
                                qk_hi(hp, g, s - 2)
                            if att:
                                if s < 2:
                                    v_hi(ah, ag, s)
                                exps(ah, ag, s)
                                if s >= 1:
                                    u_copy(ah, ag, s - 1)
                            if after and g == 0 and s >= 1:
                                gated_hi(s - 1)
                                if 2 <= s < 6:
                                    fw.act_hi(act, s - 2)
                            if g == 1 and not first and s in (2, 5):
                                mix_exp(hp - 1, s // 5)
                            if proj and s == 4:
                                split(hp, 3 * g + 2)
                            if g == 2 and s == 5:
                                split(hp, 9)
                        if att:
                            probT_hi(ah, ag, NT - 1)
                        if proj:
                            qk_hi(hp, g, NT - 2)
                            if g < 2:
                                split(hp, 3 * g + 3)
                                split(hp, 3 * g + 4)
                            elif not last:
                                split(hp, 10)
                                split(hp, 11)
                            if g == 2:
                                z_exp(hp, 0)
                            else:
                                v_copy(hp, g, 0)
                        if att:
                            u_copy(ah, ag, NT - 1)
                        if proj:
                            qk_hi(hp, g, NT - 1)
                        if proj and g == 2:
                            z_exp(hp, 1)
                            v_copy(hp, g, 0)
                        if proj:
                            v_copy(hp, g, 1)

                split(0, 0)
                split(0, 1)
                bodies(act, body)
                act.wait_ge(s_oz, 2 * HPAIRS)
                act.activation(h_hi[:, HPAIRS - 1, :], siluz[:], ACT.Copy).then_inc(s_ohi, 1)

            @block.vector
            def _(dve):
                def split(hp, j):
                    if j >= NCH:
                        hp, j = hp + 1, j - NCH
                    dve.wait_ge(s_whi, NCH * hp + j + 1)
                    dst, c = PLACE[j]
                    dve.tensor_tensor(dst[1][:, :, c:c + P], raw[j % 2][:], f(dst[0][:, :, c:c + P]), ALU.subtract).then_inc(s_wlo, 1)

                def turn(hp, g, s):
                    n = NT * (NG * hp + g) + s
                    dve.wait_ge(s_qkp, n + 1)
                    wait(dve, s_rot, n - 1)
                    for q in range(2):
                        table = keep.rope[:, q, s, :].unsqueeze(1).broadcast_to([P, 8, HD // 2])
                        last = dve.tensor_tensor(turned[s % 2][:, q, :].rearrange("p (n i) -> p n i", i=HD // 2),
                                                 bank_p[s % 2][:, 0:2 * P].rearrange("p (n i) -> p n i", i=HD // 2), table, ALU.mult)
                    last.then_inc(s_turn, 1)

                def qk_lo(hp, g, s):
                    n = NT * (NG * hp + g) + s
                    dve.wait_ge(s_qkhi, n + 1)
                    dve.tensor_tensor(perm3(qk[g][1][:], g, s * P, P),
                                      bank_qk[:, 0:2 * P].rearrange("p (x m r) -> p x m r", x=2, r=DILATION[g]),
                                      perm3(f(qk[g][0][:]), g, s * P, P), ALU.subtract).then_inc(s_qklo, 1)

                def v_lo(hp, g, q):
                    dve.wait_ge(s_vhi, 2 * (NG * hp + g) + q + 1)
                    dve.tensor_tensor(v[:, 4 * q:4 * q + 4, :, 1, :], bank_vo[:].rearrange("p (b e n) -> p b e n", b=4, e=2),
                                      f(v[:, 4 * q:4 * q + 4, :, 0, :]), ALU.subtract).then_inc(s_vlo, 1)

                def z_silu(hp, half):
                    n = 2 * (2 * hp + half)
                    dve.wait_ge(s_ez, 2 * hp + half + 1)
                    zs = siluz[:, half * HALF:(half + 1) * HALF]
                    dve.tensor_scalar(zs, zs, 1.0, None, ALU.add).then_inc(s_zchain, 1)
                    dve.wait_ge(s_zchain, n + 1)
                    dve.reciprocal(zs, zs).then_inc(s_zchain, 1)
                    dve.wait_ge(s_zchain, n + 2)
                    dve.tensor_tensor(zs, bank_p[half][:], zs, ALU.mult).then_inc(s_z, 1)

                def mask_and_max(hp, g, b):
                    A = NG * hp + g
                    n = NT * A + b
                    dve.wait_ge(s_sc, n + 1)
                    wait(dve, s_ptr, n - 1)
                    wait(dve, s_ust[b % 4], 16 * (2 * A + b // 4))
                    j0 = prev_blocks(g, b)[0]
                    if g == 2:
                        mask = keep.diag[:].unsqueeze(1).broadcast_to([P, 2, P])
                    else:
                        mask = keep.band[:, j0 * P:2 * P].unsqueeze(1).broadcast_to([P, 2, (2 - j0) * P])
                    dst = prob[b % 2][:, :, j0 * P:2 * P]
                    dve.tensor_tensor(dst, bank_s[:].rearrange("p (e j) -> p e j", e=2)[:, :, j0 * P:2 * P], mask, ALU.add).then_inc(s_mask, 1)
                    dve.wait_ge(s_mask, n + 1)
                    top = urow[b % 4][:, 2 * HD:2 * HD + 2]
                    dve.reduce_max(top, dst, axis=AXX).then_inc(s_max, 1)
                    dve.wait_ge(s_max, n + 1)
                    dve.tensor_scalar(bias[b % 2][:], top, -SCALE, None, ALU.mult).then_inc(s_bias, 1)

                def probT_lo(hp, g, b):
                    n = NT * (NG * hp + g) + b
                    dve.wait_ge(s_pthi, n + 1)
                    j0 = prev_blocks(g, b)[0]
                    hi, lo = (w[:].rearrange("p (e j) n -> p e j n", e=2)[:, :, j0:2, :] for w in probT[b % 2])
                    dve.tensor_tensor(lo, bank_pt[:].rearrange("p (e j n) -> p e j n", e=2, j=2)[:, :, j0:2, :], f(hi), ALU.subtract).then_inc(s_ptlo, 1)

                def u_add(hp, g, b):
                    n = NT * (NG * hp + g) + b
                    dve.wait_ge(s_uhi, n + 1)
                    row = urow[b % 4][:, 0:2 * HD].rearrange("p (e n) -> p e n", e=2)
                    dve.tensor_tensor(row, bank_o[:, 0:2 * P].rearrange("p (e w n) -> p e w n", e=2, w=2)[:, :, 1, :], row, ALU.add).then_inc(s_u, 1)

                def gated_lo(c, src):
                    dve.wait_ge(s_ohi, c + 1)
                    dve.tensor_tensor(h_lo[:, c, :], src, f(h_hi[:, c, :]), ALU.subtract).then_inc(s_olo, 1)

                def mix_difference(hp, q):
                    k = 2 * hp + q
                    dve.wait_ge(s_mix[q], 64 * (hp + 1))
                    mg = mix[q][:, :, 2 * HD:2 * HD + 2].rearrange("p (t g) e -> p t g e", g=NG)
                    dve.tensor_tensor(mmax[:], mg[:, :, 0, :], mg[:, :, 1, :], ALU.max).then_inc(s_mc, 1)
                    dve.wait_ge(s_mc, 6 * k + 1)
                    dve.tensor_tensor(mmax[:], mmax[:], mg[:, :, 2, :], ALU.max).then_inc(s_mc, 1)
                    dve.wait_ge(s_mc, 6 * k + 2)
                    dve.tensor_tensor(mw[:], mg, mmax[:].unsqueeze(2).broadcast_to([P, 4, NG, 2]), ALU.subtract).then_inc(s_md, 1)

                def mix_coefficients(hp, q):
                    k = 2 * hp + q
                    dve.wait_ge(s_mw, k + 1)
                    wait(dve, s_mm, k)
                    sg = mix[q][:, :, 2 * HD + 2:2 * HD + 4].rearrange("p (t g) e -> p t g e", g=NG)
                    dve.tensor_tensor(msw[:], mw[:], sg, ALU.mult).then_inc(s_mc, 1)
                    dve.wait_ge(s_mc, 6 * k + 3)
                    dve.tensor_tensor(mden[:], msw[:, :, 0, :], msw[:, :, 1, :], ALU.add).then_inc(s_mc, 1)
                    dve.wait_ge(s_mc, 6 * k + 4)
                    dve.tensor_tensor(mden[:], mden[:], msw[:, :, 2, :], ALU.add).then_inc(s_mc, 1)
                    dve.wait_ge(s_mc, 6 * k + 5)
                    dve.reciprocal(mden[:], mden[:]).then_inc(s_mc, 1)
                    dve.wait_ge(s_mc, 6 * k + 6)
                    dve.tensor_tensor(msw[:], mw[:], mden[:].unsqueeze(2).broadcast_to([P, 4, NG, 2]), ALU.mult).then_inc(s_mcoef, 1)

                def gate(hp, q):
                    dve.wait_ge(s_ot, 2 * hp + q + 1)
                    c = slice(q * HALF, (q + 1) * HALF)
                    dve.tensor_tensor(siluz[:, c], bank_vo[:], siluz[:, c], ALU.mult).then_inc(s_oz, 1)

                def unit_before(hp, g):
                    return (hp - 1, 2) if g == 0 else (hp, g - 1)

                def body(hp, first=False, last=False, after=False):
                    proj = not after
                    for g in range(NG if proj else 2):
                        att = not (first and g == 0) and not (after and g > 0)
                        ah, ag = unit_before(hp, g)
                        for s in range(NT):
                            if att and s >= 1:
                                probT_lo(ah, ag, s - 1)
                            if att:
                                mask_and_max(ah, ag, s)
                            if proj and s >= 2:
                                qk_lo(hp, g, s - 2)
                            if att:
                                if s < 2:
                                    v_lo(ah, ag, s)
                            if proj:
                                turn(hp, g, s)
                            if att and s >= 1:
                                u_add(ah, ag, s - 1)
                            if after and g == 0 and s >= 1:
                                gated_lo(s - 1, raw[(s - 1) % 2][:].rearrange("p k n -> p (k n)"))
                                if 2 <= s < 6:
                                    fw.dve_lo(dve, s - 2)
                            if g == 1 and not first:
                                if s in (2, 5):
                                    mix_difference(hp - 1, s // 5)
                                if s in (3, 6):
                                    mix_coefficients(hp - 1, s // 6)
                            if proj and s == 4:
                                split(hp, 3 * g + 2)
                            if g == 2 and s == 5:
                                split(hp, 9)
                        if att:
                            probT_lo(ah, ag, NT - 1)
                        if proj:
                            qk_lo(hp, g, NT - 2)
                            if g < 2:
                                split(hp, 3 * g + 3)
                                split(hp, 3 * g + 4)
                            elif not last:
                                split(hp, 10)
                                split(hp, 11)
                        if att:
                            u_add(ah, ag, NT - 1)
                        if proj:
                            qk_lo(hp, g, NT - 1)
                        if g == 1 and not first:
                            gate(hp - 1, 0)
                            gate(hp - 1, 1)
                        if g == 2:
                            z_silu(hp, 0)
                            z_silu(hp, 1)

                split(0, 0)
                split(0, 1)
                bodies(dve, body)
                gated_lo(HPAIRS - 1, siluz[:])
        m.clear()


def tail(nc, a, keep, l):
    h_hi, h_lo = keep.h
    x = keep.x
    w_out = (a.attn_w_out if l == 0 else a.conv_w_out)[0].rearrange("(k p) c -> p k c", p=P)
    w_gate = a.ple_w_gate[l].rearrange("(k p) c -> p k c", p=P)
    with ExitStack() as ctx:
        m = Memory(nc, ctx, f"t{l}")
        raw = [m.sb(f"raw{i}", [P, 2, HALF]) for i in range(2)]
        w = [keep.w, [m.sb(f"w1_{n}", [P, KC, HALF], F32R) for n in ("hi", "lo")]]
        y0 = m.sb("y0", [P, NT, HALF])
        gain = m.sb("gain", [P, DM])
        scratch = m.sb("scratch", [P, HALF])
        ssq = m.sb("ssq", [P, 2, NT])
        rstd = m.sb("rstd", [P, NT])
        part = [m.sb(f"part{i}", [P, HALF]) for i in range(2)]
        pp = [m.sb(f"pp{i}", [P, HALF]) for i in range(2)]
        gated = [m.sb(f"gated{i}", [P, HALF]) for i in range(2)]
        bank_y = [m.ps(f"bank_y{i}") for i in range(4)]
        bank_t = [m.ps(f"bank_t{i}") for i in range(2)]

        s_gain = m.sem("gain_in")
        s_x = m.sem("x_in")
        s_raw = [m.sem(f"raw_in{i}") for i in range(2)]
        s_whi = m.sem("w_hi_done")
        s_wlo = m.sem("w_lo_done")
        s_y = m.sem("tile_multiplied")
        s_free = m.sem("y0_bank_read")
        s_sq = m.sem("ssq_done")
        s_var = m.sem("var_chain")
        s_rstd = m.sem("rstd_done")
        s_part = m.sem("update_ready")
        s_yread = m.sem("y1_bank_read")
        s_x1 = m.sem("x_updated")
        s_xt = m.sem("x_transposed")
        s_xhi = m.sem("x_hi_done")
        s_xlo = m.sem("x_lo_done")
        s_pp = [m.sem(f"pp_in{i}") for i in range(2)]
        s_sig = m.sem("sigmoid_done")
        s_gated = m.sem("gated")
        s_x2 = m.sem("x_final")
        s_out = m.sem("out_stored")
        if l == 0:
            pair = lambda i: y0[:, 2 * i:2 * i + 2, :].rearrange("p a n -> p (a n)")
            pn = PreNorm(m, x, gain, keep.h, bank_t, keep.ident, keep.minus_half[:, 0:1], [pair(i) for i in range(3)])

        with nc.Block() as block:
            @block.sync
            def _(sp):
                sp.dma_start(x[:], (a.x[0] if l == 0 else a.xs).rearrange("(t p) c -> p t c", p=P)).then_inc(s_x, 16)
                sp.dma_start(gain[:], a.post_norm_g[l, :].partition_broadcast(P)).then_inc(s_gain, 16)

                def product(n):
                    half, t = n // NT, n % NT
                    if n >= 2:
                        sp.wait_ge(s_gated, n - 1)
                    sp.dma_start(pp[n % 2][:], a.pp[l, t * P:(t + 1) * P, half * HALF:(half + 1) * HALF]).then_inc(s_pp[n % 2], 16)

                product(0)
                product(1)
                for n in range(2 * NT):
                    if n >= 2:
                        product(n)
                    if n >= NT:
                        t = n - NT
                        sp.wait_ge(s_x2, n + 1)
                        sp.dma_start((a.out[0] if l else a.xs)[t * P:(t + 1) * P, :], x[:, t, :]).then_inc(s_out, 16)
                    elif n == 2 and l == 0:
                        sp.wait_ge(s_x1, NT)
                        sp.dma_start(gain[:], a.pre_norm_g[1, :].partition_broadcast(P)).then_inc(s_gain, 16)
                sp.wait_ge(s_out, 16 * NT)

            @block.gpsimd
            def _(pool):
                def load(n):
                    j, c = n // 4, n % 4
                    if n >= 6:
                        pool.wait_ge(s_wlo, n - 5)
                    src = (w_out if j < 2 else w_gate)[:, 2 * c:2 * c + 2, (j % 2) * HALF:(j % 2 + 1) * HALF]
                    pool.dma_start(raw[n % 2][:], src).then_inc(s_raw[n % 2], 16)

                for n in range(4, 10):
                    load(n)
                for t in range(NT):
                    c = slice(t, t + 1)
                    pool.wait_ge(s_sq, t + 1)
                    pool.tensor_tensor(rstd[:, c], ssq[:, 0, c], ssq[:, 1, c], ALU.add).then_inc(s_var, 1)
                    pool.wait_ge(s_var, 2 * t + 1)
                    pool.tensor_scalar(rstd[:, c], rstd[:, c], 1.0 / DM, RMS_EPS, ALU.mult, ALU.add).then_inc(s_var, 1)
                    pool.wait_ge(s_var, 2 * t + 2)
                    pool.tensor_tensor(rstd[:, c], rstd[:, c], keep.minus_half[:, 0:1], ALU.pow).then_inc(s_rstd, 1)
                    if t % 2 == 0:
                        load(10 + t // 2)
                for n in range(14, 16):
                    load(n)
                if l == 0:
                    for t in range(NT):
                        pn.pool_rstd(pool, t)

            @block.tensor
            def _(pe):
                def product(j, t):
                    n = NT * j + t
                    if n >= 4:
                        if n - 4 < NT:
                            pe.wait_ge(s_free, n - 3)
                        elif n - 4 < 2 * NT:
                            pe.wait_ge(s_yread, n - 4 - NT + 1)
                        else:
                            pe.wait_ge(s_sig, n - 4 - 2 * NT + 1)
                    if t == 0 and j >= 1:
                        pe.wait_ge(s_wlo, 4 * j)
                    if j == 2:
                        pe.wait_ge(s_xlo, 2 * t + 2)
                    for k in range(KC):
                        last = three_passes(pe, bank_y[n % 4][:], h_hi[:, k, t * P:(t + 1) * P], h_lo[:, k, t * P:(t + 1) * P],
                                            w[j % 2][0][:, k, :], w[j % 2][1][:, k, :], first=k == 0, last=k == KC - 1)
                    last.then_inc(s_y, 1)

                def transpose_x(t):
                    pe.wait_ge(s_x1, t + 1)
                    for half in range(2):
                        n = 2 * t + half
                        if n >= 2:
                            pe.wait_ge(s_xlo, n - 1)
                        for k in range(4):
                            c = 4 * half + k
                            last = pe.transpose(bank_t[half][:, k * P:(k + 1) * P], x[:, t, c * P:(c + 1) * P], keep.ident[:])
                        last.then_inc(s_xt, 1)

                for t in range(NT):
                    product(0, t)
                for t in range(NT):
                    product(1, t)
                    if t >= 1:
                        transpose_x(t - 1)
                product(2, 0)
                transpose_x(NT - 1)
                for t in range(1, NT):
                    product(2, t)
                for t in range(NT):
                    product(3, t)
                    if l == 0 and t >= 2:
                        pn.pe_transposes(pe, t - 2)
                if l == 0:
                    for t in range(NT - 2, NT):
                        pn.pe_transposes(pe, t)

            @block.scalar
            def _(act):
                def split(n):
                    j, c = n // 4, n % 4
                    act.wait_ge(s_raw[n % 2], 16 * (n // 2 - 1))
                    if j >= 2:
                        act.wait_ge(s_y, NT * (j - 1))
                    act.activation(w[j % 2][0][:, 2 * c:2 * c + 2, :], raw[n % 2][:], ACT.Copy).then_inc(s_whi, 1)

                def x_hi(t):
                    for half in range(2):
                        act.wait_ge(s_xt, 2 * t + half + 1)
                        act.activation(h_hi[:, 4 * half:4 * half + 4, t * P:(t + 1) * P],
                                       bank_t[half][:].rearrange("p (k n) -> p k n", k=4), ACT.Copy).then_inc(s_xhi, 1)

                def norm_behind(n):
                    t = n - NT - 1
                    if t < NT:
                        act.wait_ge(s_x2, n)
                        pn.act_squares(act, t)
                    if t >= 1:
                        pn.act_hi(act, t - 1)

                for t in range(NT):
                    if t % 2 == 0:
                        split(4 + t // 2)
                    act.wait_ge(s_y, t + 1)
                    act.activation(y0[:, t, :], bank_y[t % 4][:], ACT.Copy)
                    wait(act, s_free, t)
                    act.activation(scratch[:], bank_y[t % 4][:], ACT.Square, accum_out=ssq[:, 0, t:t + 1]).then_inc(s_free, 1)
                for t in range(NT):
                    if t % 2 == 0:
                        split(8 + t // 2)
                    act.wait_ge(s_y, NT + t + 1)
                    act.wait_ge(*((s_sq, t) if t else (s_free, NT)))
                    act.activation(scratch[:], bank_y[t % 4][:], ACT.Square, accum_out=ssq[:, 1, t:t + 1]).then_inc(s_sq, 1)
                    if t >= 1:
                        x_hi(t - 1)
                x_hi(NT - 1)
                for n in range(2 * NT):
                    if n < NT and n % 2 == 0:
                        split(12 + n // 2)
                    act.wait_ge(s_y, 2 * NT + n + 1)
                    if n >= 2:
                        act.wait_ge(s_x2, n - 1)
                    act.activation(gated[n % 2][:], bank_y[n % 4][:], ACT.Sigmoid).then_inc(s_sig, 1)
                    if l == 0 and n > NT:
                        norm_behind(n)
                if l == 0:
                    norm_behind(2 * NT)
                    norm_behind(2 * NT + 1)

            @block.vector
            def _(dve):
                def split(n):
                    j, c = n // 4, n % 4
                    dve.wait_ge(s_whi, n - 3)
                    dve.tensor_tensor(w[j % 2][1][:, 2 * c:2 * c + 2, :], raw[n % 2][:], f(w[j % 2][0][:, 2 * c:2 * c + 2, :]),
                                      ALU.subtract).then_inc(s_wlo, 1)

                def x_lo(t):
                    for half in range(2):
                        dve.wait_ge(s_xhi, 2 * t + half + 1)
                        sl = (slice(None), slice(4 * half, 4 * half + 4), slice(t * P, (t + 1) * P))
                        dve.tensor_tensor(h_lo[sl], bank_t[half][:].rearrange("p (k n) -> p k n", k=4), f(h_hi[sl]), ALU.subtract).then_inc(s_xlo, 1)

                def norm_behind(n):
                    t = n - NT - 1
                    if t == 0:
                        dve.wait_ge(s_gain, 32)
                    if t < NT:
                        pn.dve_scale(dve, t)
                    if t >= 1:
                        pn.dve_lo(dve, t - 1)

                for c in range(4):
                    split(4 + c)
                dve.wait_ge(s_gain, 16)
                dve.wait_ge(s_x, 16)
                for t in range(NT):
                    if t % 2 == 0:
                        split(8 + t // 2)
                    dve.wait_ge(s_rstd, t + 1)
                    wait(dve, s_x1, t)
                    r = rstd[:, t:t + 1]
                    dve.scalar_tensor_tensor(part[1][:], bank_y[t % 4][:], r, gain[:, HALF:DM], ALU.mult, ALU.mult).then_inc(s_yread, 1)
                    dve.scalar_tensor_tensor(part[0][:], y0[:, t, :], r, gain[:, 0:HALF], ALU.mult, ALU.mult).then_inc(s_part, 1)
                    dve.wait_ge(s_yread, t + 1)
                    dve.tensor_tensor(x[:, t, HALF:DM], x[:, t, HALF:DM], part[1][:], ALU.add)
                    dve.wait_ge(s_part, t + 1)
                    dve.tensor_tensor(x[:, t, 0:HALF], x[:, t, 0:HALF], part[0][:], ALU.add).then_inc(s_x1, 1)
                    if t >= 1:
                        x_lo(t - 1)
                x_lo(NT - 1)
                for n in range(2 * NT):
                    if n < NT and n % 2 == 0:
                        split(12 + n // 2)
                    half, t = n // NT, n % NT
                    dve.wait_ge(s_sig, n + 1)
                    dve.wait_ge(s_pp[n % 2], 16 * (n // 2 + 1))
                    dve.tensor_tensor(gated[n % 2][:], gated[n % 2][:], pp[n % 2][:], ALU.mult).then_inc(s_gated, 1)
                    dve.wait_ge(s_gated, n + 1)
                    c = slice(half * HALF, (half + 1) * HALF)
                    dve.tensor_tensor(x[:, t, c], x[:, t, c], gated[n % 2][:], ALU.add).then_inc(s_x2, 1)
                    if l == 0 and n > NT:
                        norm_behind(n)
                if l == 0:
                    norm_behind(2 * NT)
                    norm_behind(2 * NT + 1)
        if l == 0:
            m.clear()


ACT_TAPS = tuple(range(11))
DVE_TAPS = tuple(range(len(ACT_TAPS), TAPS))


def conv(nc, a, keep):
    h_hi, h_lo = keep.h
    cv = keep.x
    PAD = TAPS - 1
    COL = (DM, 0, 2 * DM)
    NW = len(COL)
    w_in = a.conv_w_in[0].rearrange("(k p) c -> p k c", p=P)
    with ExitStack() as ctx:
        m = Memory(nc, ctx, "cv")
        raw = [m.sb(f"raw{i}", [P, KC, P]) for i in range(NW)]
        w = [[b[:, :, i * P:(i + 1) * P] for b in keep.w] for i in range(NW)]
        u = [m.sb(f"u{i}", [P, PAD + SEQ]) for i in range(2)]
        sig = [m.sb(f"sig{i}", [P, HALF]) for i in range(2)]
        zsig = [m.sb(f"zsig{i}", [P, HALF]) for i in range(2)]
        zout = [m.sb(f"zout{i}", [P, HALF]) for i in range(2)]
        tap = [m.sb(f"tap{i}", [P, SEQ]) for i in range(2)]
        acc = [m.sb(f"acc{i}", [P, SEQ]) for i in range(2)]
        dacc = [m.sb(f"dacc{i}", [P, SEQ]) for i in range(2)]
        cw = [m.sb(f"cw{i}", [P, TAPS + 3]) for i in range(2)]
        mean_of = m.sb("mean_of", [P, P])
        rsum = m.sb("rsum", [P, NT])
        bank = [[m.ps(f"bank_{n}{i}") for i in range(2)] for n in "baz"]
        bank_m = [m.ps(f"bank_m{i}") for i in range(2)]

        s_raw = [m.sem(f"raw_in{i}") for i in range(NW)]
        s_ask = m.sem("buffer_free")
        s_pad = m.sem("pads_zero")
        s_cw = m.sem("channel_weights")
        s_whi = m.sem("w_hi_done")
        s_wlo = m.sem("w_lo_done")
        s_p = [m.sem(f"{n}_projected") for n in "baz"]
        s_sig = m.sem("sigmoid_b_done")
        s_zsig = m.sem("sigmoid_z_done")
        s_z = m.sem("silu_z_done")
        s_zst = [m.sem(f"silu_z_stored{i}") for i in range(2)]
        s_u = m.sem("u_done")
        s_dtap = m.sem("dve_taps")
        s_atap = m.sem("act_taps")
        s_acc0 = m.sem("acc_started")
        s_padd = m.sem("pool_adds")
        s_cv = m.sem("conv_done")
        s_mean = m.sem("mean_added")
        NA, ND = len(ACT_TAPS), len(DVE_TAPS)

        def bodies(eng, body):
            body(0)
            with eng.Fori(1, KC // 2 - 1) as i:
                body(i)
            body(KC // 2 - 1, last=True)

        def chunk(c):
            return cv[:, bass.ds(c, 1), :].rearrange("p o n -> p (o n)")

        with nc.Block() as block:
            @block.sync
            def _(sp):
                def load(c, j):
                    wait(sp, s_wlo, NW * (c - 1) + j + 1)
                    sp.sem_inc(s_ask, 1)
                    sp.dma_start(raw[j][:], w_in[:, :, bass.ds(c * P + COL[j], P)]).then_inc(s_raw[j], 16)

                def store_z(c, half):
                    wait(sp, s_z, 2 * c + half + 1)
                    sp.sem_inc(s_ask, 1)
                    sp.dma_start(a.oz[bass.ds(c * P, P), half * HALF:(half + 1) * HALF], zout[half][:]).then_inc(s_zst[half], 16)

                def body(i, last=False):
                    for q in range(2):
                        c = 2 * i + q
                        if not (last and q == 1):
                            for j in range(NW):
                                load(c + 1, j)
                        for half in range(2):
                            store_z(c, half)

                for j in range(NW):
                    load(0, j)
                bodies(sp, body)
                for half in range(2):
                    sp.wait_ge(s_zst[half], 16 * KC)

            @block.gpsimd
            def _(pool):
                for q in range(2):
                    pool.memset(u[q][:, 0:PAD], 0.0).then_inc(s_pad, 1)
                pool.memset(mean_of[:], 1.0 / DM).then_inc(s_pad, 1)

                def body(i, last=False):
                    for q in range(2):
                        c = 2 * i + q
                        for k in range(1, NA):
                            if k == 1:
                                pool.wait_ge(s_acc0, c + 1)
                            pool.wait_ge(s_atap, (NA - 1) * c + k)
                            wait(pool, s_padd, (NA - 1) * c + k - 1)
                            pool.tensor_tensor(acc[q][:], acc[q][:], tap[k % 2][:], ALU.add).then_inc(s_padd, 1)

                bodies(pool, body)

            @block.tensor
            def _(pe):
                def project(c, j):
                    pe.wait_ge(s_wlo, NW * c + j + 1)
                    for half in range(2):
                        wait(pe, (s_sig, s_u, s_z)[j], 2 * (c - 1) + half + 1)
                        for k in range(KC):
                            last = three_passes(pe, bank[j][half][:], w[j][0][:, k, :], w[j][1][:, k, :],
                                                h_hi[:, k, half * HALF:(half + 1) * HALF], h_lo[:, k, half * HALF:(half + 1) * HALF],
                                                first=k == 0, last=k == KC - 1)
                        last.then_inc(s_p[j], 1)

                def mean(c, first=False, last=False):
                    pe.wait_ge(s_cv, c + 1)
                    for half in range(2):
                        op = pe.matmul(bank_m[half][:], mean_of[:], cv[:, bass.ds(c, 1), half * HALF:(half + 1) * HALF].rearrange("p o n -> p (o n)"),
                                       start=first, stop=last)
                    op.then_inc(s_mean, 1)

                def body(i, last=False):
                    for q in range(2):
                        c = 2 * i + q
                        for j in range(NW):
                            project(c, j)
                        if not (isinstance(c, int) and c == 0):
                            mean(c - 1, first=isinstance(c, int) and c == 1)

                pe.wait_ge(s_pad, 3)
                bodies(pe, body)
                mean(KC - 1, last=True)

            @block.scalar
            def _(act):
                def split(c, j):
                    act.wait_ge(s_raw[j], 16 * (c + 1))
                    wait(act, s_p[j], 2 * c)
                    act.activation(w[j][0], raw[j][:], ACT.Copy).then_inc(s_whi, 1)

                def body(i, last=False):
                    for q in range(2):
                        c = 2 * i + q
                        more = not (last and q == 1)
                        for half in range(2):
                            act.wait_ge(s_p[0], 2 * c + half + 1)
                            wait(act, s_u, 2 * (c - 1) + half + 1)
                            act.activation(sig[half][:], bank[0][half][:], ACT.Sigmoid).then_inc(s_sig, 1)
                        if more:
                            split(c + 1, 0)
                        act.wait_ge(s_u, 2 * c + 2)
                        if more:
                            split(c + 1, 1)
                        act.wait_ge(s_cw, c + 1)
                        for n, k in enumerate(ACT_TAPS):
                            dst = acc[q] if n == 0 else tap[n % 2]
                            if n == 0:
                                wait(act, s_cv, c - 1)
                            elif n == 1 or n == 2:
                                wait(act, s_padd, (NA - 1) * c)
                            else:
                                act.wait_ge(s_padd, (NA - 1) * c + n - 2)
                            act.activation(dst[:], u[q][:, k:k + SEQ], ACT.Copy, scale=cw[q][:, k:k + 1]).then_inc(s_acc0 if n == 0 else s_atap, 1)
                            if n == NA // 2:
                                for half in range(2):
                                    act.wait_ge(s_p[2], 2 * c + half + 1)
                                    wait(act, s_z, 2 * (c - 1) + half + 1)
                                    act.activation(zsig[half][:], bank[2][half][:], ACT.Sigmoid).then_inc(s_zsig, 1)
                                if more:
                                    split(c + 1, 2)

                for j in range(NW):
                    split(0, j)
                bodies(act, body)

            @block.vector
            def _(dve):
                def split(c, j):
                    dve.wait_ge(s_whi, NW * c + j + 1)
                    dve.tensor_tensor(w[j][1], raw[j][:], f(w[j][0]), ALU.subtract).then_inc(s_wlo, 1)

                def body(i, last=False):
                    for q in range(2):
                        c = 2 * i + q
                        more = not (last and q == 1)
                        wait(dve, s_atap, (NA - 1) * (c - 1))
                        dve.tensor_copy(cw[q][:], keep.chan[:, bass.ds(c, 1), :].rearrange("p o n -> p (o n)")).then_inc(s_cw, 1)
                        if more:
                            split(c + 1, 0)
                        for half in range(2):
                            dve.wait_ge(s_p[1], 2 * c + half + 1)
                            dve.wait_ge(s_sig, 2 * c + half + 1)
                            dve.tensor_tensor(u[q][:, PAD + half * HALF:PAD + (half + 1) * HALF], bank[1][half][:], sig[half][:], ALU.mult).then_inc(s_u, 1)
                        if more:
                            split(c + 1, 1)
                        dve.wait_ge(s_u, 2 * c + 2)
                        dve.wait_ge(s_cw, c + 1)
                        dst = dacc[q][:]
                        wait(dve, s_cv, c - 1)
                        for n, k in enumerate(DVE_TAPS):
                            src = u[q][:, k:k + SEQ]
                            if n == 0:
                                dve.tensor_scalar(dst, src, cw[q][:, k:k + 1], cw[q][:, TAPS:TAPS + 1], ALU.mult, ALU.add).then_inc(s_dtap, 1)
                            else:
                                dve.wait_ge(s_dtap, ND * c + n)
                                dve.scalar_tensor_tensor(dst, src, cw[q][:, k:k + 1], dst, ALU.mult, ALU.add).then_inc(s_dtap, 1)
                            if n == ND // 2:
                                for half in range(2):
                                    dve.wait_ge(s_zsig, 2 * c + half + 1)
                                    wait(dve, s_zst[half], 16 * c)
                                    dve.tensor_tensor(zout[half][:], bank[2][half][:], zsig[half][:], ALU.mult).then_inc(s_z, 1)
                                if more:
                                    split(c + 1, 2)
                        dve.wait_ge(s_dtap, ND * (c + 1))
                        dve.wait_ge(s_padd, (NA - 1) * (c + 1))
                        dve.tensor_tensor(chunk(c), dst, acc[q][:], ALU.add).then_inc(s_cv, 1)

                for j in range(NW):
                    split(0, j)
                dve.wait_ge(s_pad, 2)
                bodies(dve, body)

        n_d = m.sem("centred")
        n_sq = m.sem("squared")
        n_sqm = m.sem("squares_added")
        n_diag = m.sem("variance_diagonal")
        n_v = m.sem("variance")
        n_eps = m.sem("variance_eps")
        n_pow = m.sem("rstd_done")
        n_rd = m.sem("rstd_diagonal")
        n_rb = m.sem("rstd_spread")
        n_zin = [m.sem(f"silu_z_in{i}") for i in range(6)]
        n_t = m.sem("normalised")
        n_s = m.sem("ln_silu_done")
        n_g = m.sem("gated")
        n_hi = m.sem("gated_hi_done")
        n_lo = m.sem("gated_lo_done")
        diag, z_in = acc[0], zout + zsig + sig
        NZ = len(z_in)
        fw = FirstWeights(m, a.conv_w_out[0], keep.w, [b[:].rearrange("p a b -> p (a b)").rearrange("p (k n) -> p k n", k=2) for b in raw]
                          + [dacc[0][:].rearrange("p (k n) -> p k n", k=2)])
        var_bank, rstd_bank = bank[0], bank[1]
        steps = [(half, c) for half in range(2) for c in range(KC)]

        def part(buf, half):
            return buf[:, half * HALF:(half + 1) * HALF]

        with nc.Block() as block:
            @block.sync
            def _(sp):
                for n, (half, c) in enumerate(steps):
                    if n >= NZ:
                        sp.wait_ge(n_g, n - NZ + 1)
                    sp.dma_start(z_in[n % NZ][:], part(a.oz[c * P:(c + 1) * P, :], half)).then_inc(n_zin[n % NZ], 16)

            @block.tensor
            def _(pe):
                for c in range(KC):
                    pe.wait_ge(n_sq, c + 1)
                    for half in range(2):
                        last = pe.matmul(var_bank[half][:], mean_of[:], part(tap[c % 2], half), start=c == 0, stop=c == KC - 1)
                    last.then_inc(n_sqm, 1)
                pe.wait_ge(n_rd, 1)
                for half in range(2):
                    last = pe.matmul(rstd_bank[half][:], mean_of[:], part(diag, half), start=True, stop=True)
                last.then_inc(n_rb, 1)

            @block.scalar
            def _(act):
                for c in range(KC):
                    act.wait_ge(n_d, c + 1)
                    if c >= 2:
                        act.wait_ge(n_sqm, c - 1)
                    act.activation(tap[c % 2][:], cv[:, c, :], ACT.Square).then_inc(n_sq, 1)
                    if c >= 4:
                        fw.act_hi(act, c - 4)

                def hi(n):
                    half, c = steps[n]
                    act.wait_ge(n_g, n + 1)
                    act.activation(part(h_hi[:, c, :], half), part(cv[:, c, :], half), ACT.Copy).then_inc(n_hi, 1)

                for n, (half, c) in enumerate(steps):
                    act.wait_ge(n_t, n + 1)
                    act.activation(part(cv[:, c, :], half), part(cv[:, c, :], half), ACT.Silu, bias=keep.chan[:, c, TAPS + 2:TAPS + 3],
                                   scale=keep.chan[:, c, TAPS + 1:TAPS + 2]).then_inc(n_s, 1)
                    if n >= 2:
                        hi(n - 2)
                for n in range(len(steps) - 2, len(steps)):
                    hi(n)

            @block.gpsimd
            def _(pool):
                def gate(n):
                    half, c = steps[n]
                    pool.wait_ge(n_s, n + 1)
                    pool.wait_ge(n_zin[n % NZ], 16 * (n // NZ + 1))
                    pool.tensor_tensor(part(cv[:, c, :], half), part(cv[:, c, :], half), z_in[n % NZ][:], ALU.mult).then_inc(n_g, 1)

                fw.load(pool)
                pool.wait_ge(n_v, 1)
                pool.tensor_scalar(rsum[:], rsum[:], 1.0, LN_EPS, ALU.mult, ALU.add).then_inc(n_eps, 1)
                pool.wait_ge(n_eps, 1)
                pool.tensor_tensor(rsum[:], rsum[:], keep.minus_half[:, 0:1].broadcast_to([P, NT]), ALU.pow).then_inc(n_pow, 1)
                for n in range(len(steps)):
                    gate(n)

            @block.vector
            def _(dve):
                for c in range(KC):
                    for half in range(2):
                        last = dve.tensor_tensor(part(cv[:, c, :], half), part(cv[:, c, :], half), bank_m[half][:], ALU.subtract)
                    last.then_inc(n_d, 1)
                for n in range(4):
                    fw.dve_lo(dve, n)
                dve.wait_ge(n_sqm, KC)
                dview = diag[:].rearrange("p (t n) -> p t n", n=P)
                for half in range(2):
                    last = dve.tensor_tensor(dview[:, 4 * half:4 * half + 4, :], var_bank[half][:].rearrange("p (t n) -> p t n", n=P),
                                             keep.ident[:].unsqueeze(1).broadcast_to([P, 4, P]), ALU.mult)
                last.then_inc(n_diag, 1)
                dve.wait_ge(n_diag, 1)
                dve.reduce_sum(rsum[:], dview, axis=AXX).then_inc(n_v, 1)
                dve.wait_ge(n_pow, 1)
                dve.tensor_scalar(rsum[:], rsum[:], float(DM), None, ALU.mult).then_inc(n_diag, 1)
                dve.wait_ge(n_diag, 2)
                dve.tensor_tensor(dview, keep.ident[:].unsqueeze(1).broadcast_to([P, NT, P]), rsum[:].unsqueeze(2).broadcast_to([P, NT, P]), ALU.mult).then_inc(n_rd, 1)
                dve.wait_ge(n_rb, 1)

                def normalise(n):
                    half, c = steps[n]
                    dve.tensor_tensor(part(cv[:, c, :], half), part(cv[:, c, :], half), rstd_bank[half][:], ALU.mult).then_inc(n_t, 1)

                def lo(n):
                    half, c = steps[n]
                    dve.wait_ge(n_hi, n + 1)
                    dve.tensor_tensor(part(h_lo[:, c, :], half), part(cv[:, c, :], half), f(part(h_hi[:, c, :], half)), ALU.subtract).then_inc(n_lo, 1)

                for n in range(len(steps) + 3):
                    if n < len(steps):
                        normalise(n)
                    if n >= 3:
                        lo(n - 3)
        m.clear()


class Tensors:
    pass


def build(nc, a):
    with ExitStack() as ctx:
        keep = Tensors()
        m = Memory(nc, ctx, "all")
        keep.h = [m.sb(f"h_{n}", [P, KC, SEQ], F32R) for n in ("hi", "lo")]
        keep.ident = m.sb("ident", [P, P])
        keep.minus_half = m.sb("minus_half", [P, 1])
        keep.chan = m.sb("chan", [P, KC, TAPS + 3])
        keep.band = m.sb("band", [P, 2 * P])
        keep.diag = m.sb("diag", [P, P])
        keep.rope = m.sb("rope", [P, 2, NT, HD // 2])
        setup(nc, a, keep)
        keep.w = [m.sb(f"w_{n}", [P, KC, HALF], F32R) for n in ("hi", "lo")]
        attention(nc, a, keep)
        keep.x = m.sb("x", [P, NT, DM])
        tail(nc, a, keep, 0)
        conv(nc, a, keep)
        tail(nc, a, keep, 1)


_INS = ["x", "p", "positions", "pre_norm_g", "post_norm_g", "attn_w_in", "attn_w_out", "conv_w_in", "conv_dw_w",
        "conv_dw_b", "conv_ln_g", "conv_ln_b", "conv_w_out", "ple_w_proj", "ple_w_gate"]


def kernel(**inputs):
    from concourse import bacc
    from concourse.bass_utils import run_bass_kernel_spmd

    nc = bacc.Bacc("TRN2", target_bir_lowering=False, num_devices=1)
    a = Tensors()
    arrays = {}
    for name in _INS:
        arrays[name] = np.ascontiguousarray(inputs[name])
    dram = lambda name, shape, dt, kind: nc.dram_tensor(name, shape, dt, kind=kind).ap()
    a.x, a.p, a.positions, a.pre_norm_g, a.post_norm_g, a.attn_w_in, a.attn_w_out, a.conv_w_in, a.conv_dw_w, \
        a.conv_dw_b, a.conv_ln_g, a.conv_ln_b, a.conv_w_out, a.ple_w_proj, a.ple_w_gate = (
            dram(n, arrays[n].shape, mybir.dt.from_np(arrays[n].dtype), "ExternalInput") for n in _INS)
    a.u = dram("groups_out", (HPAIRS, NG, SEQ, UROW), F32, "Internal")
    a.oz = dram("gated_out", (DM, SEQ), F32, "Internal")
    a.xs = dram("x_between", (SEQ, DM), F32, "Internal")
    a.pp = dram("ple_products", (2, SEQ, DM), F32, "Internal")
    a.out = dram("result", (1, SEQ, DM), F32, "ExternalOutput")
    build(nc, a)
    r = run_bass_kernel_spmd(nc, [arrays], core_ids=[0])
    return r.results[0]["result"]
```
